# Optimizing a Trainium2 kernel written in Bass

```python
import jax, jax.numpy as jnp
from jax import lax
import numpy as np
import math

D_MODEL = 1024
BATCH = 1
SEQ = 256
DEPTH = 1

N_MEM = 256
EPS = 1e-6
FOX_HEADS = 8
FOX_HEAD_DIM = 64
FOX_WIDTH = FOX_HEADS * FOX_HEAD_DIM
Q_BLOCK = 128
GDN_HEADS = 4
GDN_HEAD_DIM = 128
GDN_WIDTH = GDN_HEADS * GDN_HEAD_DIM
CONV_WIDTH = 4
CHUNK = 64
MIX_WIDTH = FOX_WIDTH + GDN_WIDTH
IN_PROJ_SIZES = (FOX_WIDTH, FOX_WIDTH, FOX_WIDTH, FOX_HEADS,
                 GDN_WIDTH, GDN_WIDTH, GDN_WIDTH, GDN_WIDTH, GDN_HEADS, GDN_HEADS)
IN_PROJ_WIDTH = sum(IN_PROJ_SIZES)
SPLIT_POINTS = tuple(np.cumsum(IN_PROJ_SIZES)[:-1].tolist())
MEM_HEADS = 4
MEM_HEAD_DIM = D_MODEL // MEM_HEADS
D_FF = 2816
FFN_RESIDUAL_WEIGHT = 0.5


def rms_norm(x, gain):
    xf = x.astype(jnp.float32)
    y = xf * lax.rsqrt(jnp.mean(xf * xf, axis=-1, keepdims=True) + EPS)
    return (y * gain.astype(jnp.float32)).astype(x.dtype)

def l2_norm(x):
    return x * lax.rsqrt(jnp.sum(x * x, axis=-1, keepdims=True) + EPS)

def swiglu(x, w_gate, w_up, w_down):
    return (jax.nn.silu(x @ w_gate) * (x @ w_up)) @ w_down

def forgetting_attention(q, k, v, f_logit):
    B, S, H, Dh = q.shape
    nb = S // Q_BLOCK
    F = jnp.cumsum(jax.nn.log_sigmoid(f_logit.astype(jnp.float32)), axis=1).transpose(0, 2, 1)
    qb = (q * (Dh ** -0.5)).reshape(B, nb, Q_BLOCK, H, Dh).transpose(1, 0, 3, 2, 4)
    Fq = F.reshape(B, H, nb, Q_BLOCK).transpose(2, 0, 1, 3)
    q_pos = jnp.arange(S).reshape(nb, Q_BLOCK)
    k_pos = jnp.arange(S)

    def block(args):
        q_blk, F_blk, pos_blk = args
        s = jnp.einsum('bhqd,bshd->bhqs', q_blk, k, preferred_element_type=jnp.float32)
        s = s + F_blk[..., None] - F[:, :, None, :]
        s = jnp.where(pos_blk[:, None] >= k_pos[None, :], s, -jnp.inf)
        p = jax.nn.softmax(s, axis=-1).astype(v.dtype)
        return jnp.einsum('bhqs,bshd->bqhd', p, v)

    out = lax.map(block, (qb, Fq, q_pos))
    return out.transpose(1, 0, 2, 3, 4).reshape(B, S, H * Dh)

def causal_conv_silu(x, w):
    S = x.shape[1]
    xp = jnp.pad(x, ((0, 0), (CONV_WIDTH - 1, 0), (0, 0)))
    y = xp[:, 0:S] * w[0]
    for i in range(1, CONV_WIDTH):
        y = y + xp[:, i:i + S] * w[i]
    return jax.nn.silu(y)

def gated_delta_rule_chunked(q, k, v, g, beta):
    B, S, H, Dk = q.shape
    Dv = v.shape[-1]
    n = S // CHUNK

    def chunks(t):
        return t.reshape(B, n, CHUNK, H, -1).transpose(0, 3, 1, 2, 4)

    q = chunks(q) * (Dk ** -0.5)
    k = chunks(k)
    v = chunks(v)
    beta = beta.reshape(B, n, CHUNK, H).transpose(0, 3, 1, 2)
    g = jnp.cumsum(g.reshape(B, n, CHUNK, H).transpose(0, 3, 1, 2), axis=-1)
    k_beta = k * beta[..., None]
    v_beta = v * beta[..., None]
    incl = jnp.tril(jnp.ones((CHUNK, CHUNK), dtype=bool))
    strict = jnp.tril(jnp.ones((CHUNK, CHUNK), dtype=bool), -1)
    decay = jnp.exp(jnp.where(incl, g[..., :, None] - g[..., None, :], -jnp.inf))
    L = jnp.where(strict, jnp.einsum('bhncd,bhnsd->bhncs', k_beta, k) * decay, 0.0)
    A = L + jnp.eye(CHUNK, dtype=L.dtype)
    u = lax.linalg.triangular_solve(A, v_beta, left_side=True, lower=True)
    w = lax.linalg.triangular_solve(A, k_beta * jnp.exp(g)[..., None], left_side=True, lower=True)
    attn_intra = jnp.einsum('bhncd,bhnsd->bhncs', q, k) * decay
    q_decay = q * jnp.exp(g)[..., None]
    g_last = g[..., -1]
    k_tail = k * jnp.exp(g_last[..., None] - g)[..., None]

    def step(state, xs):
        w_c, u_c, qd_c, a_c, kt_c, gl_c = xs
        v_new = u_c - jnp.einsum('bhcd,bhde->bhce', w_c, state)
        o = jnp.einsum('bhcd,bhde->bhce', qd_c, state) + jnp.einsum('bhcs,bhse->bhce', a_c, v_new)
        state = state * jnp.exp(gl_c)[..., None, None] + jnp.einsum('bhcd,bhce->bhde', kt_c, v_new)
        return state, o

    xs = (jnp.moveaxis(w, 2, 0), jnp.moveaxis(u, 2, 0), jnp.moveaxis(q_decay, 2, 0),
          jnp.moveaxis(attn_intra, 2, 0), jnp.moveaxis(k_tail, 2, 0), jnp.moveaxis(g_last, 2, 0))
    state0 = jnp.zeros((B, H, Dk, Dv), jnp.float32)
    _, o = lax.scan(step, state0, xs)
    return o.transpose(1, 0, 3, 2, 4).reshape(B, S, H, Dv)

def hybrid_mixer(u, w_in, fox_f_bias, gdn_conv_w, gdn_a_log, gdn_dt_bias, gdn_out_norm):
    B, S, _ = u.shape
    proj = u @ w_in
    fq, fk, fv, ff, gq, gk, gv, gz, gb, ga = jnp.split(proj, SPLIT_POINTS, axis=-1)
    fox = forgetting_attention(fq.reshape(B, S, FOX_HEADS, FOX_HEAD_DIM),
                               fk.reshape(B, S, FOX_HEADS, FOX_HEAD_DIM),
                               fv.reshape(B, S, FOX_HEADS, FOX_HEAD_DIM),
                               ff + fox_f_bias)
    qkv = causal_conv_silu(jnp.concatenate([gq, gk, gv], axis=-1).astype(jnp.float32),
                           gdn_conv_w.astype(jnp.float32))
    cq, ck, cv = jnp.split(qkv, (GDN_WIDTH, 2 * GDN_WIDTH), axis=-1)
    q = l2_norm(cq.reshape(B, S, GDN_HEADS, GDN_HEAD_DIM))
    k = l2_norm(ck.reshape(B, S, GDN_HEADS, GDN_HEAD_DIM))
    v = cv.reshape(B, S, GDN_HEADS, GDN_HEAD_DIM)
    beta = jax.nn.sigmoid(gb.astype(jnp.float32))
    g = -jnp.exp(gdn_a_log.astype(jnp.float32)) * jax.nn.softplus(
        ga.astype(jnp.float32) + gdn_dt_bias.astype(jnp.float32))
    o = gated_delta_rule_chunked(q, k, v, g, beta)
    o = rms_norm(o, gdn_out_norm) * jax.nn.silu(
        gz.astype(jnp.float32).reshape(B, S, GDN_HEADS, GDN_HEAD_DIM))
    gdn = o.reshape(B, S, GDN_WIDTH).astype(u.dtype)
    return jnp.concatenate([fox.astype(u.dtype), gdn], axis=-1)

def memory_cross_attention(h, m, w_q, w_kv, w_o):
    B, S, _ = h.shape
    q = (h @ w_q).reshape(B, S, MEM_HEADS, MEM_HEAD_DIM)
    k, v = jnp.split(m @ w_kv, 2, axis=-1)
    k = k.reshape(B, -1, MEM_HEADS, MEM_HEAD_DIM)
    v = v.reshape(B, -1, MEM_HEADS, MEM_HEAD_DIM)
    s = jnp.einsum('bqhd,bmhd->bhqm', q, k, preferred_element_type=jnp.float32) * (MEM_HEAD_DIM ** -0.5)
    p = jax.nn.softmax(s, axis=-1).astype(v.dtype)
    o = jnp.einsum('bhqm,bmhd->bqhd', p, v).reshape(B, S, D_MODEL)
    return o @ w_o

def first_inputs(seed: int = 0) -> dict:
    key = jax.random.key(seed)
    ks = iter(jax.random.split(key, 40))

    def normal(shape, scale):
        return jax.random.normal(next(ks), shape, jnp.float32) * scale

    def gain(width):
        return 1.0 + normal((DEPTH, width), 0.02)

    L = DEPTH
    dt = jnp.exp(jax.random.uniform(next(ks), (L, GDN_HEADS), jnp.float32,
                                    minval=float(np.log(1e-3)), maxval=float(np.log(1e-1))))
    return {
        'x': normal((BATCH, SEQ, D_MODEL), 1.0),
        'mem': normal((BATCH, N_MEM, D_MODEL), 1.0),
        'ffn1_pre_norm': gain(D_MODEL),
        'ffn1_w_gate': normal((L, D_MODEL, D_FF), D_MODEL ** -0.5),
        'ffn1_w_up': normal((L, D_MODEL, D_FF), D_MODEL ** -0.5),
        'ffn1_w_down': normal((L, D_FF, D_MODEL), D_FF ** -0.5),
        'ffn1_post_norm': gain(D_MODEL),
        'mix_pre_norm': gain(D_MODEL),
        'w_in': normal((L, D_MODEL, IN_PROJ_WIDTH), D_MODEL ** -0.5),
        'fox_f_bias': jax.random.uniform(next(ks), (L, FOX_HEADS), jnp.float32, minval=1.0, maxval=4.0),
        'gdn_conv_w': normal((L, CONV_WIDTH, 3 * GDN_WIDTH), CONV_WIDTH ** -0.5),
        'gdn_a_log': jnp.log(jax.random.uniform(next(ks), (L, GDN_HEADS), jnp.float32, minval=1.0, maxval=16.0)),
        'gdn_dt_bias': dt + jnp.log(-jnp.expm1(-dt)),
        'gdn_out_norm': gain(GDN_HEAD_DIM),
        'w_out': normal((L, MIX_WIDTH, D_MODEL), MIX_WIDTH ** -0.5),
        'mix_post_norm': gain(D_MODEL),
        'mem_pre_norm': gain(D_MODEL),
        'mem_kv_norm': gain(D_MODEL),
        'mem_w_q': normal((L, D_MODEL, D_MODEL), D_MODEL ** -0.5),
        'mem_w_kv': normal((L, D_MODEL, 2 * D_MODEL), D_MODEL ** -0.5),
        'mem_w_o': normal((L, D_MODEL, D_MODEL), D_MODEL ** -0.5),
        'mem_post_norm': gain(D_MODEL),
        'ffn2_pre_norm': gain(D_MODEL),
        'ffn2_w_gate': normal((L, D_MODEL, D_FF), D_MODEL ** -0.5),
        'ffn2_w_up': normal((L, D_MODEL, D_FF), D_MODEL ** -0.5),
        'ffn2_w_down': normal((L, D_FF, D_MODEL), D_FF ** -0.5),
        'ffn2_post_norm': gain(D_MODEL),
    }

def first_block(x, mem, ffn1_pre_norm, ffn1_w_gate, ffn1_w_up, ffn1_w_down, ffn1_post_norm,
              mix_pre_norm, w_in, fox_f_bias, gdn_conv_w, gdn_a_log, gdn_dt_bias, gdn_out_norm,
              w_out, mix_post_norm, mem_pre_norm, mem_kv_norm, mem_w_q, mem_w_kv, mem_w_o,
              mem_post_norm, ffn2_pre_norm, ffn2_w_gate, ffn2_w_up, ffn2_w_down, ffn2_post_norm):
    h = x
    for l in range(DEPTH):
        f = swiglu(rms_norm(h, ffn1_pre_norm[l]), ffn1_w_gate[l], ffn1_w_up[l], ffn1_w_down[l])
        h = h + FFN_RESIDUAL_WEIGHT * rms_norm(f, ffn1_post_norm[l])
        mixed = hybrid_mixer(rms_norm(h, mix_pre_norm[l]), w_in[l], fox_f_bias[l], gdn_conv_w[l],
                             gdn_a_log[l], gdn_dt_bias[l], gdn_out_norm[l])
        h = h + rms_norm(mixed @ w_out[l], mix_post_norm[l])
        c = memory_cross_attention(rms_norm(h, mem_pre_norm[l]), rms_norm(mem, mem_kv_norm[l]),
                                   mem_w_q[l], mem_w_kv[l], mem_w_o[l])
        h = h + rms_norm(c, mem_post_norm[l])
        f = swiglu(rms_norm(h, ffn2_pre_norm[l]), ffn2_w_gate[l], ffn2_w_up[l], ffn2_w_down[l])
        h = h + FFN_RESIDUAL_WEIGHT * rms_norm(f, ffn2_post_norm[l])
    return h


CONV_WIDTH_2 = D_MODEL
CONV_TAPS = 31
DIFF_HEADS = 8
DIFF_HEAD_DIM = 64
DIFF_V_DIM = 2 * DIFF_HEAD_DIM
QK_WIDTH = DIFF_HEADS * 2 * DIFF_HEAD_DIM
ATTN_WIDTH = DIFF_HEADS * DIFF_V_DIM
ROPE_THETA = 500000.0
ROPE_DIM = DIFF_HEAD_DIM // 4
IN_SIZES = (CONV_WIDTH_2, CONV_WIDTH_2, QK_WIDTH, QK_WIDTH, ATTN_WIDTH, D_MODEL, D_MODEL)
IN_WIDTH = 2 * CONV_WIDTH_2 + 2 * QK_WIDTH + ATTN_WIDTH + 2 * D_MODEL
N_EXPERTS = 64
N_GROUPS = 8
TOPK_GROUPS = 4
TOP_K = 8
EXPERT_DIM = 256
SHARED_DIM = 256
ROUTED_SCALE = 2.5
MOE_CHUNK = 128


def rms_norm_2(x, g):
    x32 = x.astype(jnp.float32)
    y = x32 * lax.rsqrt(jnp.mean(x32 * x32, axis=-1, keepdims=True) + EPS)
    return y.astype(x.dtype) * g

def layer_norm(x, g, b):
    x32 = x.astype(jnp.float32)
    mu = jnp.mean(x32, axis=-1, keepdims=True)
    xc = x32 - mu
    y = xc * lax.rsqrt(jnp.mean(xc * xc, axis=-1, keepdims=True) + EPS)
    return y.astype(x.dtype) * g + b

def rope(x, cos, sin):
    half = ROPE_DIM // 2
    x1, x2, xp = x[..., :half], x[..., half:ROPE_DIM], x[..., ROPE_DIM:]
    return jnp.concatenate([x1 * cos - x2 * sin, x2 * cos + x1 * sin, xp], axis=-1)

def conformer_conv(a, b, w_dw, b_dw, ln_g, ln_b, w_pw2, b_pw2):
    u = a * jax.nn.sigmoid(b)
    u = lax.conv_general_dilated(
        u, w_dw[:, None, :], window_strides=(1,), padding=[(CONV_TAPS - 1, 0)],
        dimension_numbers=('NWC', 'WIO', 'NWC'), feature_group_count=CONV_WIDTH_2) + b_dw
    u = jax.nn.silu(layer_norm(u, ln_g, ln_b))
    return u @ w_pw2 + b_pw2

def diff_attention(q, k, v, cos, sin, q_g, k_g, lq1, lk1, lq2, lk2, subln_g, lambda_init):
    B, S, _ = q.shape
    H, d = DIFF_HEADS, DIFF_HEAD_DIM
    q = q.reshape(B, S, H, 2, d).transpose(0, 2, 3, 1, 4)
    k = k.reshape(B, S, H, 2, d).transpose(0, 2, 3, 1, 4)
    v = v.reshape(B, S, H, DIFF_V_DIM).transpose(0, 2, 1, 3)
    q = rope(rms_norm_2(q, q_g), cos, sin)
    k = rope(rms_norm_2(k, k_g), cos, sin)
    f32 = jnp.float32
    lam = (jnp.exp(jnp.sum(lq1.astype(f32) * lk1.astype(f32)))
           - jnp.exp(jnp.sum(lq2.astype(f32) * lk2.astype(f32))) + lambda_init)
    nb = S // Q_BLOCK
    q_blocks = jnp.moveaxis(q.reshape(B, H, 2, nb, Q_BLOCK, d), 3, 0)
    starts = jnp.arange(nb, dtype=jnp.int32) * Q_BLOCK
    k_idx = jnp.arange(S, dtype=jnp.int32)
    scale = d ** -0.5

    def block(args):
        qb, start = args
        s = jnp.einsum('bhmqd,bhmkd->bhmqk', qb, k).astype(f32) * scale
        causal = k_idx[None, :] <= (start + jnp.arange(Q_BLOCK, dtype=jnp.int32))[:, None]
        p = jax.nn.softmax(jnp.where(causal, s, -jnp.inf), axis=-1)
        a = p[:, :, 0] - lam * p[:, :, 1]
        return jnp.einsum('bhqk,bhkv->bhqv', a.astype(v.dtype), v)

    o = lax.map(block, (q_blocks, starts))
    o = jnp.moveaxis(o, 0, 2).reshape(B, H, S, DIFF_V_DIM)
    o = rms_norm_2(o, subln_g) * (1.0 - lambda_init)
    return o.transpose(0, 2, 1, 3).reshape(B, S, ATTN_WIDTH)

def moe_ffn(h, w_router, router_bias, w_gu, w_down, w_sh_gu, w_sh_down):
    B, S, D = h.shape
    f32 = jnp.float32
    t = h.reshape(B * S, D)
    scores = jax.nn.sigmoid((t @ w_router).astype(f32))
    choice = scores + router_bias.astype(f32)
    per_group = N_EXPERTS // N_GROUPS
    group_score = lax.top_k(choice.reshape(-1, N_GROUPS, per_group), 2)[0].sum(-1)
    _, gidx = lax.top_k(group_score, TOPK_GROUPS)
    gmask = jax.nn.one_hot(gidx, N_GROUPS, dtype=f32).sum(-2)
    emask = jnp.repeat(gmask, per_group, axis=-1) > 0
    _, eidx = lax.top_k(jnp.where(emask, choice, -jnp.inf), TOP_K)
    w = jnp.take_along_axis(scores, eidx, axis=-1)
    w = w / jnp.sum(w, axis=-1, keepdims=True) * ROUTED_SCALE
    gates = jnp.einsum('tk,tke->te', w, jax.nn.one_hot(eidx, N_EXPERTS, dtype=f32)).astype(h.dtype)
    nc = t.shape[0] // MOE_CHUNK

    def chunk(args):
        tc, gc = args
        g, u = jnp.split(jnp.einsum('td,edf->tef', tc, w_gu), 2, axis=-1)
        return jnp.einsum('tef,efd->td', jax.nn.silu(g) * u * gc[..., None], w_down)

    routed = lax.map(chunk, (t.reshape(nc, MOE_CHUNK, D),
                             gates.reshape(nc, MOE_CHUNK, N_EXPERTS))).reshape(B * S, D)
    sg, su = jnp.split(t @ w_sh_gu, 2, axis=-1)
    shared = (jax.nn.silu(sg) * su) @ w_sh_down
    return (routed + shared).reshape(B, S, D)

def second_inputs(seed: int = 0) -> dict:
    key = jax.random.key(seed)
    ks = jax.random.split(key, 32)
    L, D, C = DEPTH, D_MODEL, CONV_WIDTH_2
    f32 = jnp.float32

    def nrm(k, shape, scale):
        return jax.random.normal(k, shape, f32) * scale

    def gain(k, shape):
        return 1.0 + 0.05 * jax.random.normal(k, shape, f32)

    return {
        'x': nrm(ks[0], (BATCH, SEQ, D), 1.0),
        'c': nrm(ks[1], (BATCH, D), 1.0),
        'positions': jnp.broadcast_to(jnp.arange(SEQ, dtype=jnp.int32), (BATCH, SEQ)),
        'w_ada': nrm(ks[2], (L, D, 6 * D), 0.5 * D ** -0.5),
        'b_ada': nrm(ks[3], (L, 6 * D), 0.02),
        'norm1_g': gain(ks[4], (L, D)),
        'w_in': nrm(ks[5], (L, D, IN_WIDTH), D ** -0.5),
        'conv_dw': nrm(ks[6], (L, CONV_TAPS, C), CONV_TAPS ** -0.5),
        'conv_dw_b': nrm(ks[7], (L, C), 0.02),
        'conv_ln_g': gain(ks[8], (L, C)),
        'conv_ln_b': nrm(ks[9], (L, C), 0.02),
        'w_pw2': nrm(ks[10], (L, C, D), C ** -0.5),
        'b_pw2': nrm(ks[11], (L, D), 0.02),
        'q_norm_g': gain(ks[12], (L, DIFF_HEAD_DIM)),
        'k_norm_g': gain(ks[13], (L, DIFF_HEAD_DIM)),
        'lambda_q1': nrm(ks[14], (L, DIFF_HEAD_DIM), 0.1),
        'lambda_k1': nrm(ks[15], (L, DIFF_HEAD_DIM), 0.1),
        'lambda_q2': nrm(ks[16], (L, DIFF_HEAD_DIM), 0.1),
        'lambda_k2': nrm(ks[17], (L, DIFF_HEAD_DIM), 0.1),
        'subln_g': gain(ks[18], (L, DIFF_V_DIM)),
        'w_out': nrm(ks[19], (L, D, D), D ** -0.5),
        'norm2_g': gain(ks[20], (L, D)),
        'w_router': nrm(ks[21], (L, D, N_EXPERTS), D ** -0.5),
        'router_bias': nrm(ks[22], (L, N_EXPERTS), 0.01),
        'w_exp_gu': nrm(ks[23], (L, N_EXPERTS, D, 2 * EXPERT_DIM), D ** -0.5),
        'w_exp_down': nrm(ks[24], (L, N_EXPERTS, EXPERT_DIM, D), EXPERT_DIM ** -0.5),
        'w_sh_gu': nrm(ks[25], (L, D, 2 * SHARED_DIM), D ** -0.5),
        'w_sh_down': nrm(ks[26], (L, SHARED_DIM, D), SHARED_DIM ** -0.5),
    }

def second_block(x, c, positions, w_ada, b_ada, norm1_g, w_in, conv_dw, conv_dw_b, conv_ln_g,
              conv_ln_b, w_pw2, b_pw2, q_norm_g, k_norm_g, lambda_q1, lambda_k1, lambda_q2,
              lambda_k2, subln_g, w_out, norm2_g, w_router, router_bias, w_exp_gu, w_exp_down,
              w_sh_gu, w_sh_down):
    inv_freq = ROPE_THETA ** (-jnp.arange(0, ROPE_DIM, 2, dtype=jnp.float32) / ROPE_DIM)
    ang = positions.astype(jnp.float32)[:, None, None, :, None] * inv_freq
    cos = jnp.cos(ang).astype(x.dtype)
    sin = jnp.sin(ang).astype(x.dtype)
    c_act = jax.nn.silu(c)
    offsets = []
    acc = 0
    for s in IN_SIZES[:-1]:
        acc += s
        offsets.append(acc)
    for l in range(DEPTH):
        lambda_init = 0.8 - 0.6 * math.exp(-0.3 * l)
        mod = c_act @ w_ada[l] + b_ada[l]
        sh1, sc1, g1, sh2, sc2, g2 = [m[:, None, :] for m in jnp.split(mod, 6, axis=-1)]
        h = rms_norm_2(x, norm1_g[l]) * (1 + sc1) + sh1
        proj = h @ w_in[l]
        ca, cb, q, k, v, gate_conv, gate_attn = jnp.split(proj, offsets, axis=-1)
        y_conv = conformer_conv(ca, cb, conv_dw[l], conv_dw_b[l], conv_ln_g[l], conv_ln_b[l],
                                w_pw2[l], b_pw2[l])
        y_attn = diff_attention(q, k, v, cos, sin, q_norm_g[l], k_norm_g[l], lambda_q1[l],
                                lambda_k1[l], lambda_q2[l], lambda_k2[l], subln_g[l], lambda_init)
        merged = jax.nn.sigmoid(gate_conv) * y_conv + jax.nn.sigmoid(gate_attn) * y_attn
        x = x + g1 * (merged @ w_out[l])
        h2 = rms_norm_2(x, norm2_g[l]) * (1 + sc2) + sh2
        x = x + g2 * moe_ffn(h2, w_router[l], router_bias[l], w_exp_gu[l], w_exp_down[l],
                             w_sh_gu[l], w_sh_down[l])
    return x


def setup_inputs(seed=0):
    out = dict(first_inputs(seed))
    for name, value in second_inputs(seed + 1).items():
        if name != "x":
            out[name + "_2"] = value
    return out


def reference(
    x, mem, ffn1_pre_norm, ffn1_w_gate, ffn1_w_up, ffn1_w_down, ffn1_post_norm, mix_pre_norm,
    w_in, fox_f_bias, gdn_conv_w, gdn_a_log, gdn_dt_bias, gdn_out_norm, w_out, mix_post_norm,
    mem_pre_norm, mem_kv_norm, mem_w_q, mem_w_kv, mem_w_o, mem_post_norm, ffn2_pre_norm,
    ffn2_w_gate, ffn2_w_up, ffn2_w_down, ffn2_post_norm, c_2, positions_2, w_ada_2, b_ada_2,
    norm1_g_2, w_in_2, conv_dw_2, conv_dw_b_2, conv_ln_g_2, conv_ln_b_2, w_pw2_2, b_pw2_2,
    q_norm_g_2, k_norm_g_2, lambda_q1_2, lambda_k1_2, lambda_q2_2, lambda_k2_2, subln_g_2,
    w_out_2, norm2_g_2, w_router_2, router_bias_2, w_exp_gu_2, w_exp_down_2, w_sh_gu_2,
    w_sh_down_2,
):
    x = first_block(
        x, mem, ffn1_pre_norm, ffn1_w_gate, ffn1_w_up, ffn1_w_down, ffn1_post_norm,
        mix_pre_norm, w_in, fox_f_bias, gdn_conv_w, gdn_a_log, gdn_dt_bias, gdn_out_norm, w_out,
        mix_post_norm, mem_pre_norm, mem_kv_norm, mem_w_q, mem_w_kv, mem_w_o, mem_post_norm,
        ffn2_pre_norm, ffn2_w_gate, ffn2_w_up, ffn2_w_down, ffn2_post_norm,
    )
    return second_block(
        x, c_2, positions_2, w_ada_2, b_ada_2, norm1_g_2, w_in_2, conv_dw_2, conv_dw_b_2,
        conv_ln_g_2, conv_ln_b_2, w_pw2_2, b_pw2_2, q_norm_g_2, k_norm_g_2, lambda_q1_2,
        lambda_k1_2, lambda_q2_2, lambda_k2_2, subln_g_2, w_out_2, norm2_g_2, w_router_2,
        router_bias_2, w_exp_gu_2, w_exp_down_2, w_sh_gu_2, w_sh_down_2,
    )


_drawn_inputs = setup_inputs


def setup_inputs(seed=0):
    import zlib

    import numpy as np

    out = dict(_drawn_inputs(seed))
    spreads = {}
    factors = {'ffn1_post_norm': 3.338,
     'gdn_out_norm': 3.304,
     'mix_post_norm': 2.901,
     'mem_pre_norm': 3.858,
     'mem_kv_norm': 2.733,
     'mem_post_norm': 3.343,
     'ffn2_pre_norm': 4.346,
     'ffn2_post_norm': 6.842,
     'norm1_g_2': 6.874,
     'conv_dw_b_2': 64.0,
     'conv_ln_g_2': 43.695,
     'conv_ln_b_2': 64.0,
     'b_pw2_2': 64.0,
     'q_norm_g_2': 8.0,
     'k_norm_g_2': 8.0,
     'lambda_q1_2': 64.0,
     'lambda_k1_2': 64.0,
     'lambda_q2_2': 8.0,
     'lambda_k2_2': 8.0,
     'subln_g_2': 39.775,
     'norm2_g_2': 6.784,
     'router_bias_2': 8.0}
    for name, (base, spread) in spreads.items():
        noise = np.random.default_rng([zlib.crc32(name.encode()), seed]).standard_normal(out[name].shape)
        drawn = base * np.exp(spread * noise) if base else spread * noise
        out[name] = __import__('jax').numpy.asarray(drawn.astype(out[name].dtype))
    for name, factor in factors.items():
        out[name] = (out[name] * factor).astype(out[name].dtype)
    return out
```

```python
from contextlib import ExitStack
import math

import numpy as np

import concourse.bass as bass
from concourse import mybir

F32 = mybir.dt.float32
I32 = mybir.dt.int32
ALU = mybir.AluOpType
ACT = mybir.ActivationFunctionType
AX = mybir.AxisListType

P = 128
D = 1024
DC = D // P
S = 256
T = S // P
EPS = 1e-6
D_FF = 2816
FB = 256
NF = D_FF // FB
N_EXP = 64
NS = 4
SLOT = DC * 512 + 2 * D
LOADS = 3
PEEL = 2
STAGES = "ABCDEF"
NEG = -1e30
LEVELS = 6
ARENA = 16448


class Steps:

    def __init__(self, eng, own):
        self.eng, self.own, self.count = eng, own, {}

    def __call__(self, ins, sem=None):
        sem = self.own if sem is None else sem
        self.count[sem.name] = self.count.get(sem.name, 0) + 1
        ins.then_inc(sem, 1)
        self.eng.wait_ge(sem, self.count[sem.name])


class Queue:

    def __init__(self, eng, full, free):
        self.eng, self.full, self.free, self.n = eng, full, free, 0

    def fill(self):
        if self.n >= 8:
            self.eng.wait_ge(self.free, self.n - 7)
        self.n += 1
        return (self.n - 1) % 8

    def take(self):
        self.n += 1
        self.eng.wait_ge(self.full, self.n)
        return (self.n - 1) % 8

    def emptied(self):
        if self.n:
            self.eng.wait_ge(self.free, self.n)


def rounds(eng, n, peel):
    for a in range(min(peel, n)):
        yield a, 0
    loops = (n - peel) // NS
    if loops > 0:
        with eng.Fori(0, loops) as j:
            for u in range(NS):
                yield peel + u, j
    for a in range(peel + max(loops, 0) * NS, n):
        yield a, 0


def build(nc, A, out):
    with ExitStack() as ctx:
        program(nc, A, out, ctx)


def program(nc, A, out, ctx):
    sems = {}

    def sem(name):
        if name not in sems:
            sems[name] = ctx.enter_context(nc.semaphore(name))
        return sems[name]

    def sb(name, shape, dt=F32):
        return ctx.enter_context(nc.sbuf_tensor(name, shape, dt))

    ring = [sb(f"ring{i}", [P, SLOT]) for i in range(NS)]
    wide = [r[:, 0:DC * 512].rearrange("p (c n) -> p c n", c=DC) for r in ring]
    down = [r[:, DC * 512:SLOT].rearrange("p (f n) -> p f n", f=2) for r in ring]
    h = sb("h", [P, T, D])
    xn = sb("xn", [P, T, D])
    xT = sb("xT", [P, DC, S])
    ident = sb("ident", [P, P])
    tri1 = sb("tri1", [P, 2 * P])
    tri, ones = tri1[:, 0:P], tri1[:, P:2 * P]
    tri_chunk = sb("tri_chunk", [P, P])
    ones_chunk = sb("ones_chunk", [P, P])
    causal = sb("causal", [P, P])
    causal_chunk = sb("causal_chunk", [P, P])
    levels = sb("levels", [P, LEVELS, P])
    earlier = sb("earlier", [P, 8, 8])
    eps = sb("eps", [P, 1])
    stat = sb("stat", [P, 32])
    sm = sb("sm", [P, 528])
    gainb = [sb(f"gainb{i}", [P, D]) for i in range(2)]
    preg = sb("preg", [P, 5, DC])
    arena = sb("arena", [P, ARENA])
    ps = [ctx.enter_context(nc.psum_tensor(f"bank{i}", [P, 512], F32)) for i in range(8)]
    gates_dram = nc.dram_tensor("gates_by_expert", [N_EXP, S], F32).ap()

    def view(t, start, shape):
        v = t[:, start:start + int(np.prod(shape))]
        names = "abcd"[:len(shape)]
        if len(shape) > 1:
            v = v.rearrange(f"p ({' '.join(names)}) -> p {' '.join(names)}",
                            **{k: s for k, s in zip(names, shape)})
        return v

    def carve(start, *shape):
        end = start + int(np.prod(shape))
        assert end <= ARENA, (start, shape)
        return view(arena, start, shape), end

    def every(ap, *shape):
        for _ in shape:
            ap = ap.unsqueeze(1)
        return ap.to_broadcast([ap.shape[0], *shape, ap.shape[-1]])

    def along(ap, n):
        ap = ap.unsqueeze(len(ap.shape))
        return ap.to_broadcast([*ap.shape[:-1], n])

    psum_full, psum_free = sem("psum_full"), sem("psum_free")
    loaded = [sem(f"slot_loaded{i}") for i in range(NS)]
    v_step, a_step, g_step = sem("vector_step"), sem("scalar_step"), sem("gpsimd_step")
    x_loaded, params_loaded, consts = sem("x_loaded"), sem("params_loaded"), sem("consts_made")
    operands_set = sem("operands_set")
    scalar_in = sem("scalar_input_set")
    scalar_out = sem("scalar_output_set")
    gain_loaded = [sem(f"gain_loaded{i}") for i in range(2)]
    gain_used = sem("gain_used")
    out_done = sem("out_done")

    release = []
    handed = []

    class Pe:
        def __init__(self, eng):
            self.eng, self.q = eng, Queue(eng, psum_full, psum_free)
            self.block = self.sets = 0

        def slot(self):
            b = self.block
            self.block += 1
            self.eng.wait_ge(loaded[b % NS], 16 * LOADS * (b // NS + 1))
            return b % NS

        def get(self):
            self.sets += 1
            self.eng.wait_ge(operands_set, self.sets)

        def released(self):
            release.append((psum_full, self.q.n))

    class Vec:
        def __init__(self, eng):
            self.eng, self.do = eng, Steps(eng, v_step)
            self.q = Queue(eng, psum_full, psum_free)
            self.outs = self.gains = 0

        def feed(self):
            self.eng.sem_inc(operands_set, 1)

        def ask(self):
            self.eng.sem_inc(scalar_in, 1)

        def answer(self):
            self.outs += 1
            self.eng.wait_ge(scalar_out, self.outs)

        def hand(self):
            b = self.q.take()
            handed.append(b)
            return b

        def give_back(self, n):
            self.eng.sem_inc(psum_free, n)
            self.do.count[psum_free.name] = self.do.count.get(psum_free.name, 0) + n

        def gain(self):
            k = self.gains
            self.gains += 1
            self.eng.wait_ge(gain_loaded[k % 2], 16 * (k // 2 + 1))
            return gainb[k % 2]

    class Act:
        def __init__(self, eng):
            self.eng, self.do = eng, Steps(eng, a_step)
            self.ins = self.hands = 0

        def get(self):
            self.ins += 1
            self.eng.wait_ge(scalar_in, self.ins)

        def put(self):
            self.eng.sem_inc(scalar_out, 1)

        def bank(self):
            self.hands += 1
            return ps[handed[self.hands - 1]]

    def act_norm(a, src):
        a.get()
        for t in range(T):
            a.do(a.eng.activation(xn[:, t], src[:, t], ACT.Square, accum_out=stat[:, t:t + 1]))
        a.do(a.eng.activation(stat[:, 2:4], stat[:, 0:2], ACT.Sqrt, bias=eps[:], scale=1.0 / D))
        a.put()

    def vec_norm(v, src):
        v.ask()
        v.answer()
        v.do(v.eng.reciprocal(stat[:, 4:6], stat[:, 2:4]))
        for t in range(T):
            v.do(v.eng.tensor_scalar(xn[:, t], src[:, t], stat[:, 4 + t:5 + t], None, ALU.mult))

    def act_bank_norm(a, banks):
        a.get()
        for t in range(T):
            for n in range(2):
                a.do(a.eng.activation(xn[:, t, n * 512:(n + 1) * 512], banks(t, n)[:],
                                      ACT.Square, accum_out=stat[:, 8 + 2 * n + t:9 + 2 * n + t]))
        for t in range(T):
            a.do(a.eng.activation(stat[:, 12 + t:13 + t], stat[:, 8 + t:9 + t],
                                  ACT.Identity, bias=stat[:, 10 + t:11 + t]))
        a.do(a.eng.activation(stat[:, 14:16], stat[:, 12:14], ACT.Sqrt, bias=eps[:],
                              scale=1.0 / D))
        a.put()

    def vec_residual(v, banks, weight):
        g = v.gain()
        v.ask()
        v.answer()
        v.do(v.eng.reciprocal(stat[:, 16:18], stat[:, 14:16]))
        v.do(v.eng.tensor_scalar(stat[:, 18:20], stat[:, 16:18], weight, None, ALU.mult))
        for t in range(T):
            for n in range(2):
                at = slice(n * 512, (n + 1) * 512)
                v.do(v.eng.scalar_tensor_tensor(xn[:, t, at], banks(t, n)[:],
                                                stat[:, 18 + t:19 + t], g[:, at],
                                                ALU.mult, ALU.mult))
        v.do(v.eng.tensor_tensor(h[:], h[:], xn[:], ALU.add))
        v.eng.sem_inc(gain_used, 1)

    def vec_to_features(v, dst, chunks, gain=None):
        for c in range(0, chunks, 2):
            b = v.q.take()
            if gain is None:
                v.do(v.eng.tensor_copy(dst[:, c:c + 2, :], view(ps[b], 0, (2, S))), psum_free)
            else:
                for k in range(2):
                    v.do(v.eng.tensor_scalar(dst[:, c + k, :], ps[b][:, k * S:(k + 1) * S],
                                             gain[:, c + k:c + k + 1], None, ALU.mult),
                         psum_free if k else None)
        v.feed()

    def pe_to_features(pe, src, chunks):
        for c in range(0, chunks, 2):
            b = pe.q.fill()
            for k in range(2):
                for t in range(T):
                    ins = pe.eng.transpose(ps[b][:, k * S + t * P:k * S + (t + 1) * P],
                                           src(c + k, t), ident[:])
            ins.then_inc(psum_full, 1)

    def strided(src):
        v = src[:].rearrange("p t (q c) -> p t c q", c=DC)
        return lambda c, t: v[:, t, c, :]

    def pe_tokens(pe, lhs, n=512, bias=None):
        w = wide[pe.slot()]
        for t in range(T):
            b = pe.q.fill()
            for c in range(DC):
                ins = pe.eng.matmul(ps[b][:, 0:n], lhs[:, c, t * P:(t + 1) * P], w[:, c, 0:n],
                                    start=c == 0, stop=c == DC - 1 and bias is None)
            if bias is not None:
                ins = pe.eng.matmul(ps[b][:, 0:n], bias[0], bias[1], start=False, stop=True)
            ins.then_inc(psum_full, 1)
        pe.released()

    def pe_features(pe, rhs):
        w = wide[pe.slot()]
        for f in range(0, 4, 2):
            b = pe.q.fill()
            for k in range(2):
                for c in range(DC):
                    ins = pe.eng.matmul(ps[b][:, k * S:(k + 1) * S],
                                        w[:, c, (f + k) * P:(f + k + 1) * P], rhs[:, c, :],
                                        start=c == 0, stop=c == DC - 1)
            ins.then_inc(psum_full, 1)
        pe.released()

    def pe_product(pe, lhs):
        for _ in range(2):
            pe_tokens(pe, lhs)

    def vec_product_residual(v, weight):
        got = [v.hand() for _ in range(4)]
        vec_residual(v, lambda t, n: ps[got[2 * n + t]], weight)
        v.give_back(4)

    def act_product_norm(a):
        got = [a.bank() for _ in range(4)]
        act_bank_norm(a, lambda t, n: got[2 * n + t])

    def weight(name):
        w = A[name]
        return w.rearrange("l d n -> (l d) n") if len(w.shape) == 3 else w

    def by_feature(name, lo, n=512, natural=False):
        how = "(c p) n -> p c n" if natural else "(p c) n -> p c n"
        return weight(name).rearrange(how, c=DC)[:, :, lo:lo + n]

    class Sp:
        def __init__(self, eng):
            self.eng, self.block = eng, 0

        def load(self, parts):
            b = self.block
            self.block += 1
            if b >= NS:
                self.eng.wait_ge(*release[b - NS])
            pairs = parts(b % NS)
            assert len(pairs) == LOADS
            for dst, src in pairs:
                self.eng.dma_start(dst, src).then_inc(loaded[b % NS], 16)

        def project(self, name, lo, n=512, natural=False):
            src = by_feature(name, lo, n, natural)
            self.load(lambda s: [(wide[s][:, a:b, 0:n], src[:, a:b, :])
                                 for a, b in ((0, 3), (3, 6), (6, 8))])

    ff_sg, ff_end = carve(0, 4, S)
    ff_h, ff_end = carve(ff_end, 2, 2, S)
    gate_rows, ff_end = carve(ff_end, NS, S)
    ff_bank = lambda t, n: ps[2 * t + n]

    def ff_sems(tag):
        return [sem(f"{tag}_{x}") for x in ("gu_full", "silu_set", "hidden_set", "down_done")]

    def pe_ff(pe, tag, n):
        gu_full, _, hidden_set, down_done = ff_sems(tag)
        base = pe.block
        pe.q.emptied()

        def second(a, j, first, last):
            s = (base + a) % NS
            pe.eng.wait_ge(hidden_set, 2 * (a + NS * j) + 2)
            for f in range(2):
                for t in range(T):
                    for m in range(2):
                        ins = pe.eng.matmul(ff_bank(t, m)[:], ff_h[:, a % 2, f, t * P:(t + 1) * P],
                                            down[s][:, f, m * 512:(m + 1) * 512],
                                            start=first and f == 0, stop=last and f == 1,
                                            skip_group_check=True)
            ins.then_inc(down_done, 1)

        for a, j in rounds(pe.eng, n, PEEL):
            s = (base + a) % NS
            pe.eng.wait_ge(loaded[s], 16 * LOADS * ((base + a) // NS + 1 + j))
            if a >= PEEL:
                pe.eng.wait_ge(hidden_set, 2 * (a + NS * j) - 2)
            for f in range(2):
                b = 4 + 2 * (a % 2) + f
                for k in range(2):
                    for c in range(DC):
                        ins = pe.eng.matmul(ps[b][:, k * S:(k + 1) * S],
                                            wide[s][:, c, k * FB + f * P:k * FB + (f + 1) * P],
                                            xT[:, c, :], start=c == 0, stop=c == DC - 1,
                                            skip_group_check=True)
                ins.then_inc(gu_full, 1)
            if a >= 1:
                second(a - 1, j, a == 1, False)
        second(n - 1, 0, False, True)
        release.extend((down_done, i + 1) for i in range(n))
        pe.block += n

    def act_ff(ac, tag, n):
        gu_full, silu_set, hidden_set, _ = ff_sems(tag)
        for a, j in rounds(ac.eng, n, PEEL):
            for f in range(2):
                i = 2 * (a + NS * j) + f
                ac.eng.wait_ge(gu_full, i + 1)
                if a >= PEEL:
                    ac.eng.wait_ge(hidden_set, i - 3)
                ac.eng.activation(ff_sg[:, (2 * a + f) % 4, :], ps[4 + 2 * (a % 2) + f][:, 0:S],
                                  ACT.Silu).then_inc(silu_set, 1)

    def vec_ff(v, tag, n, gate_loaded=None):
        _, silu_set, hidden_set, down_done = ff_sems(tag)
        gated = sem("gated_step")
        for a, j in rounds(v.eng, n, PEEL):
            with_gate = gate_loaded is not None and a >= 1
            if a >= PEEL:
                v.eng.wait_ge(down_done, a + NS * j - 1)
            if with_gate:
                v.eng.wait_ge(gate_loaded[(a - 1) % NS], 16 * ((a - 1) // NS + 1 + j))
            for f in range(2):
                i = 2 * (a + NS * j) + f
                hid = ff_h[:, a % 2, f, :]
                v.eng.wait_ge(silu_set, i + 1)
                ins = v.eng.tensor_tensor(hid, ff_sg[:, (2 * a + f) % 4, :],
                                          ps[4 + 2 * (a % 2) + f][:, S:2 * S], ALU.mult)
                if with_gate:
                    ins.then_inc(gated, 1)
                    v.eng.wait_ge(gated, i - 1)
                    ins = v.eng.tensor_tensor(hid, hid, gate_rows[:, (a - 1) % NS, :], ALU.mult)
                ins.then_inc(hidden_set, 1)
        v.eng.wait_ge(down_done, n)

    def dense(tag, gain_at):
        def pe_part(pe):
            pe.get()
            pe_to_features(pe, strided(xn), DC)
            pe.get()
            pe_ff(pe, tag, NF)

        def vec_part(v):
            vec_norm(v, h)
            v.feed()
            vec_to_features(v, xT, DC, preg[:, gain_at])
            vec_ff(v, tag, NF)
            vec_residual(v, ff_bank, 0.5)

        def act_part(a):
            act_norm(a, h)
            act_ff(a, tag, NF)
            act_bank_norm(a, ff_bank)

        def sp_part(sp):
            wg, wu = (weight(f"{tag}_w_{x}").rearrange("(p c) n -> p c n", c=DC)
                      for x in ("gate", "up"))
            wd = weight(f"{tag}_w_down").rearrange("(i f p) n -> i p f n", f=2, p=P)
            for i in range(NF):
                at = slice(i * FB, (i + 1) * FB)
                sp.load(lambda s: [(wide[s][:, :, 0:FB], wg[:, :, at]),
                                   (wide[s][:, :, FB:2 * FB], wu[:, :, at]),
                                   (down[s], wd[i])])
        return pe_part, vec_part, act_part, sp_part

    params = [(preg[:, i], A[n][0].rearrange("(p c) -> p c", c=DC)) for i, n in enumerate(
        ("ffn1_pre_norm", "mix_pre_norm", "mem_pre_norm", "mem_kv_norm", "ffn2_pre_norm"))]
    gain_order = [n for s, n in zip("ABCDEF", (
        "ffn1_post_norm", "mix_post_norm", "mem_post_norm", "ffn2_post_norm", "norm1_g_2",
        "norm2_g_2")) if s in STAGES]

    STAGE_PARTS = {"A": dense("ffn1", 0), "D": dense("ffn2", 4)}

    FH, FD = 8, 64
    GH, GD, CH = 4, 128, 64
    PAD = 3
    FK0, FV0, FF0 = 512, 1024, 1536
    GQ0 = FF0 + FH
    GZ0, GB0 = GQ0 + 3 * 512, GQ0 + 4 * 512

    def bank_heads(t, heads):
        n = 4 // (t + 1)
        return [[2 * (i + k) + half for k in range(n)]
                for i in range(0, heads // 2, n) for half in range(2)]

    def mixer():
        qkvP, e = carve(0, 12, PAD + S)
        conv, e = carve(e, 12, S)
        qkv, e = carve(e, T, 12, P)
        gz, e = carve(e, T, 512)
        fox0 = e
        fqT, e = carve(e, 4, S)
        fkT, e = carve(e, 4, S)
        fv, e = carve(e, T, 512)
        Frow = xn[:].rearrange("p t (a s) -> p (t a) s", s=S)
        soft, e = carve(e, FH * 3 * P)
        tiles = [soft[:, 0:FH * P].rearrange("p (h k) -> p h k", h=FH),
                 soft[:, FH * P:3 * FH * P].rearrange("p (h k) -> p h k", h=FH)]
        softT, _ = carve(0, 3 * FH, P)
        qT, e = carve(0, GH, S)
        kT, e = carve(e, GH, S)
        kbT, e = carve(e, GH, S)
        qdT, e = carve(e, GH, S)
        dec, e = carve(e, T, GH, P)
        LT, e = carve(e, T, GH, P)
        kb, e = carve(fox0, T, GH, P)
        kbg, e = carve(e, T, GH, P)
        kt, e = carve(e, T, GH, P)
        qd, e = carve(e, T, GH, P)
        X, e = carve(e, T, GH, P)
        XT, e = carve(e, T, GH, P)
        Mb, T1 = qd, kb
        u, wT = Mb, T1
        state = kbT[:, 0:2, :].rearrange("p a (b d) -> p (a b) d", b=2)
        o = LT
        sq = X
        mix = xn

        def small(lo, *shape):
            return view(sm, lo, shape)

        raw, neg, lsp = small(0, T, 16), small(32, T, 16), small(64, T, 16)
        fg, ea, beta = small(96, T, 12), small(120, 4), small(124, T, GH)
        cum = small(132, 32)
        Fq, G, Gend = small(132, T, FH), small(148, T, GH), small(156, T, GH)
        nG, eG, eT = small(164, T, GH), small(172, T, GH), small(180, T, GH)
        eEnd = small(188, T, 2, GH)
        mx, den, rden = small(204, T, FH), small(220, T, FH), small(236, T, FH)
        ss, rr = small(252, T, 8), small(268, T, 8)
        cw = small(300, 4, 12)
        bias16, a_log = small(350, 16), small(366, 4)
        oss, orr = small(370, T, GH), small(378, T, GH)
        cw_rows = sb("gdn_tap_rows", [12, 4, P])
        ogain = sb("gdn_gain", [P, GD])

        params.extend([
            (bias16[:, 0:8], A["fox_f_bias"][0].partition_broadcast(P)),
            (bias16[:, 12:16], A["gdn_dt_bias"][0].partition_broadcast(P)),
            (a_log, A["gdn_a_log"][0].partition_broadcast(P)),
            (ogain[:], A["gdn_out_norm"][0].partition_broadcast(P)),
            (cw_rows[:], A["gdn_conv_w"][0].rearrange("i (c p) -> c i p", p=P)),
        ])

        def pe_part(pe):
            mm, tr = pe.eng.matmul, pe.eng.transpose
            pe.get()
            pe_to_features(pe, strided(xn), DC)
            pe.get()
            w = wide[pe.slot()]
            b = pe.q.fill()
            for t in range(T):
                for c in range(DC):
                    ins = mm(ps[b][:, t * 16:(t + 1) * 16], xT[:, c, t * P:(t + 1) * P],
                             w[:, c, 0:16], start=c == 0, stop=c == DC - 1)
            ins.then_inc(psum_full, 1)
            pe.released()
            b = pe.q.fill()
            for i in range(4):
                ins = tr(ps[b][:, 12 * i:12 * i + 12], cw_rows[:, i, :], ident[0:12, 0:12])
            ins.then_inc(psum_full, 1)
            for _ in range(5):
                pe_features(pe, xT)
            for _ in range(2):
                pe_tokens(pe, xT)
            pe.get()
            b = pe.q.fill()
            mm(ps[b][:, 0:8], tri, fg[:, 0, 0:8], start=True, stop=True)
            mm(ps[b][:, 8:16], tri, fg[:, 1, 0:8], start=True, stop=False)
            mm(ps[b][:, 8:16], ones, fg[:, 0, 0:8], start=False, stop=True)
            for t in range(T):
                mm(ps[b][:, 16 + 4 * t:20 + 4 * t], tri_chunk[:], fg[:, t, 8:12],
                   start=True, stop=True)
                ins = mm(ps[b][:, 24 + 4 * t:28 + 4 * t], ones_chunk[:], fg[:, t, 8:12],
                         start=True, stop=True)
            ins.then_inc(psum_full, 1)
            for hd in range(0, FH, 2):
                b = pe.q.fill()
                for k in range(2):
                    one = fg[:, 0, hd + k:hd + k + 1].to_broadcast([P, P])
                    two = fg[:, 1, hd + k:hd + k + 1].to_broadcast([P, P])
                    mm(ps[b][:, k * S:k * S + P], one, tri, start=True, stop=True)
                    mm(ps[b][:, k * S + P:(k + 1) * S], one, ones, start=True, stop=False)
                    ins = mm(ps[b][:, k * S + P:(k + 1) * S], two, tri, start=False, stop=True)
                ins.then_inc(psum_full, 1)
            for t in range(T):
                kw = (t + 1) * P
                for heads in bank_heads(t, FH):
                    b = pe.q.fill()
                    for k, hd in enumerate(heads):
                        r = slice(FD * (hd % 2), FD * (hd % 2 + 1))
                        ins = mm(ps[b][:, k * kw:(k + 1) * kw],
                                 fqT[r, hd // 2, t * P:(t + 1) * P], fkT[r, hd // 2, 0:kw],
                                 start=True, stop=True)
                    ins.then_inc(psum_full, 1)
            pe.get()
            for t in range(T):
                for c in range(0, 12, 4):
                    b = pe.q.fill()
                    for k in range(4):
                        ins = tr(ps[b][:, k * P:(k + 1) * P], conv[:, c + k, t * P:(t + 1) * P],
                                 ident[:])
                    ins.then_inc(psum_full, 1)
            for t in range(T):
                pe.get()
                blocks = [(hd, k) for hd in range(FH) for k in range(t + 1)]
                for i in range(0, len(blocks), 4):
                    b = pe.q.fill()
                    for n, (hd, k) in enumerate(blocks[i:i + 4]):
                        ins = tr(ps[b][:, n * P:(n + 1) * P], tiles[t][:, hd, k * P:(k + 1) * P],
                                 ident[:])
                    ins.then_inc(psum_full, 1)
            pe.get()
            for t in range(T):
                b = pe.q.fill()
                for hd in range(FH):
                    for k in range(t + 1):
                        at = hd if t == 0 else FH + 2 * hd + k
                        ins = mm(ps[b][:, hd * FD:(hd + 1) * FD], softT[:, at, :],
                                 fv[:, k, hd * FD:(hd + 1) * FD], start=k == 0, stop=k == t)
                ins.then_inc(psum_full, 1)
            for t in range(T):
                b = pe.q.fill()
                for hd in range(GH):
                    ins = mm(ps[b][:, hd * P:(hd + 1) * P],
                             fg[:, t, 8 + hd:9 + hd].to_broadcast([P, P]), tri_chunk[:],
                             start=True, stop=True)
                ins.then_inc(psum_full, 1)
            pe.get()
            for src in (qkv[:, :, 0:4, :], qkv[:, :, 4:8, :], kb, qd):
                for t in range(T):
                    b = pe.q.fill()
                    for hd in range(GH):
                        ins = tr(ps[b][:, hd * P:(hd + 1) * P], src[:, t, hd, :], ident[:])
                    ins.then_inc(psum_full, 1)
            pe.get()
            for rhs in (kbT, qT):
                for t in range(T):
                    b = pe.q.fill()
                    for hd in range(GH):
                        at = slice(t * P, (t + 1) * P)
                        ins = mm(ps[b][:, hd * P:(hd + 1) * P], kT[:, hd, at], rhs[:, hd, at],
                                 start=True, stop=True)
                    ins.then_inc(psum_full, 1)

            def four(lhs, rhs):
                for t in range(T):
                    b = pe.q.fill()
                    for hd in range(GH):
                        ins = mm(ps[b][:, hd * P:(hd + 1) * P], lhs[:, t, hd, :], rhs[:, t, hd, :],
                                 start=True, stop=True)
                    ins.then_inc(psum_full, 1)

            for k in range(LEVELS):
                pe.get()
                four(Mb, X)
                pe.get()
                if k < LEVELS - 1:
                    four(XT, T1)
                four(T1, XT)
            pe.get()
            four(XT, qkv[:, :, 8:12, :])
            four(kbg, XT)
            for n in range(S // CH):
                t, r0 = n // 2, CH * (n % 2)
                r = slice(r0, r0 + CH)
                at = slice(t * P + r0, t * P + r0 + CH)
                if n:
                    pe.get()
                    b = pe.q.fill()
                    for hd in range(GH):
                        ins = mm(ps[b][r, hd * P:(hd + 1) * P], wT[:, t, hd, r], state[:, hd, :],
                                 start=True, stop=True)
                    ins.then_inc(psum_full, 1)
                pe.get()
                b = pe.q.fill()
                for hd in range(GH):
                    if n:
                        mm(ps[b][r, hd * P:(hd + 1) * P], qdT[:, hd, at], state[:, hd, :],
                           start=True, stop=False)
                    ins = mm(ps[b][r, hd * P:(hd + 1) * P], dec[r, t, hd, r], u[r, t, hd, :],
                             start=n == 0, stop=True)
                ins.then_inc(psum_full, 1)
                if n < S // CH - 1:
                    b = pe.q.fill()
                    for hd in range(GH):
                        ins = mm(ps[b][:, hd * P:(hd + 1) * P], kt[r, t, hd, :], u[r, t, hd, :],
                                 start=True, stop=True)
                    ins.then_inc(psum_full, 1)
            pe.get()
            pe_to_features(pe, strided(mix), DC)
            pe.get()
            pe_product(pe, xT)

        def vec_part(v):
            e, do = v.eng, v.do
            tt, ts, cp = e.tensor_tensor, e.tensor_scalar, e.tensor_copy
            do(e.memset(qkvP[:, :, 0:PAD], 0.0))
            do(e.memset(bias16[:, 8:12], 0.0))
            vec_norm(v, h)
            v.feed()
            vec_to_features(v, xT, DC, preg[:, 1])
            b = v.q.take()
            do(tt(raw, view(ps[b], 0, (T, 16)), every(bias16, T), ALU.add), psum_free)
            do(ts(neg, raw, -1.0, None, ALU.mult))
            do(tt(neg, raw, neg, ALU.min))
            v.ask()
            b = v.q.take()
            do(cp(cw, view(ps[b], 0, (4, 12))), psum_free)
            for c in range(0, 12, 2):
                b = v.q.take()
                do(cp(qkvP[:, c:c + 2, PAD:], view(ps[b], 0, (2, S))), psum_free)
            for c in range(0, 4, 2):
                b = v.q.take()
                do(ts(fqT[:, c:c + 2, :], view(ps[b], 0, (2, S)), FD ** -0.5, None, ALU.mult),
                   psum_free)
            for c in range(0, 4, 2):
                b = v.q.take()
                do(cp(fkT[:, c:c + 2, :], view(ps[b], 0, (2, S))), psum_free)
            for dst in (fv, gz):
                for t in range(T):
                    b = v.q.take()
                    do(cp(dst[:, t, :], ps[b][:]), psum_free)
            v.answer()
            do(ts(neg, raw, 0.0, None, ALU.min))
            do(tt(fg[:, :, 0:8], neg[:, :, 0:8], lsp[:, :, 0:8], ALU.subtract))
            do(ts(raw, raw, 0.0, None, ALU.max))
            do(tt(fg[:, :, 8:12], raw[:, :, 12:16], lsp[:, :, 12:16], ALU.add))
            do(ts(ea, ea, -1.0, None, ALU.mult))
            do(tt(fg[:, :, 8:12], fg[:, :, 8:12], every(ea, T), ALU.mult))
            v.feed()
            b = v.q.take()
            do(cp(cum, ps[b][:, 0:32]), psum_free)
            do(ts(nG, G, -1.0, None, ALU.mult))
            do(tt(eT, Gend, G, ALU.subtract))
            v.ask()
            for hd in range(0, FH, 2):
                b = v.q.take()
                do(cp(Frow[:, hd:hd + 2, :], view(ps[b], 0, (2, S))), psum_free)
            for c in range(12):
                do(ts(conv[:, c, :], qkvP[:, c, 0:S], cw[:, 0, c:c + 1], None, ALU.mult))
                for i in range(1, 4):
                    do(e.scalar_tensor_tensor(conv[:, c, :], qkvP[:, c, i:i + S],
                                              cw[:, i, c:c + 1], conv[:, c, :],
                                              ALU.mult, ALU.add))
            v.ask()
            for t in range(T):
                kw = (t + 1) * P
                for heads in bank_heads(t, FH):
                    b = v.q.take()
                    for k, hd in enumerate(heads):
                        do(e.scalar_tensor_tensor(
                            tiles[t][:, hd, :], ps[b][:, k * kw:(k + 1) * kw],
                            Fq[:, t, hd:hd + 1], Frow[:, hd, 0:kw],
                            ALU.add, ALU.subtract), psum_free if hd == heads[-1] else None)
                diag = tiles[t][:, :, t * P:kw]
                do(tt(diag, diag, every(causal[:], FH), ALU.add))
                do(e.tensor_reduce(mx[:, t], tiles[t], AX.X, ALU.max))
            do(ts(mx, mx, -1.0, None, ALU.mult))
            v.answer()
            v.answer()
            v.feed()
            v.ask()
            for t in range(T):
                for c in range(0, 12, 4):
                    b = v.q.take()
                    do(cp(qkv[:, t, c:c + 4, :], view(ps[b], 0, (4, P))), psum_free)
            for t in range(T):
                v.answer()
                v.feed()
                for i in range(0, FH * (t + 1), 4):
                    b = v.q.take()
                    do(cp(softT[:, FH * t + i:FH * t + i + 4, :], view(ps[b], 0, (4, P))),
                       psum_free)
            v.feed()
            do(e.reciprocal(rden, den))
            for t in range(T):
                b = v.q.take()
                do(tt(mix[:, t, 0:512].rearrange("p (h d) -> p h d", h=FH),
                      view(ps[b], 0, (FH, FD)), along(rden[:, t, :], FD), ALU.mult), psum_free)
            for t in range(T):
                b = v.q.take()
                do(tt(dec[:, t], view(ps[b], 0, (GH, P)), every(causal_chunk[:], GH), ALU.add))
                for n in range(2):
                    do(cp(eEnd[:, t, n, :],
                          view(ps[b], 0, (GH, P))[:, :, CH * n + CH - 1]),
                       psum_free if n else None)
            v.ask()
            do(tt(X, qkv[:, :, 0:4, :], qkv[:, :, 0:4, :], ALU.mult))
            do(e.tensor_reduce(ss[:, :, 0:4], X, AX.X, ALU.add))
            do(tt(X, qkv[:, :, 4:8, :], qkv[:, :, 4:8, :], ALU.mult))
            do(e.tensor_reduce(ss[:, :, 4:8], X, AX.X, ALU.add))
            v.ask()
            v.answer()
            v.answer()
            do(e.reciprocal(rr, ss))
            do(ts(rr[:, :, 0:4], rr[:, :, 0:4], GD ** -0.5, None, ALU.mult))
            for t in range(T):
                do(tt(qkv[:, t, 0:8, :], qkv[:, t, 0:8, :], along(rr[:, t], P), ALU.mult))
                k_, v_ = qkv[:, t, 4:8, :], qkv[:, t, 8:12, :]
                do(tt(kb[:, t], k_, along(beta[:, t], P), ALU.mult))
                do(tt(kbg[:, t], kb[:, t], along(eG[:, t], P), ALU.mult))
                do(tt(kt[:, t], k_, along(eT[:, t], P), ALU.mult))
                do(tt(qd[:, t], qkv[:, t, 0:4, :], along(eG[:, t], P), ALU.mult))
                do(tt(v_, v_, along(beta[:, t], P), ALU.mult))
            v.feed()
            for dst in (qT, kT, kbT, qdT):
                for t in range(T):
                    b = v.q.take()
                    do(cp(dst[:, :, t * P:(t + 1) * P], view(ps[b], 0, (GH, P))), psum_free)
            v.feed()
            for dst in (LT, dec):
                for t in range(T):
                    b = v.q.take()
                    do(tt(dst[:, t], view(ps[b], 0, (GH, P)), dec[:, t], ALU.mult), psum_free)
            for t in range(T):
                do(cp(X[:, t], every(ident[:], GH)))
                do(cp(XT[:, t], every(ident[:], GH)))

            def four(op):
                for t in range(T):
                    b = v.q.take()
                    do(op(t, view(ps[b], 0, (GH, P))), psum_free)

            for k in range(LEVELS):
                for t in range(T):
                    do(tt(Mb[:, t], LT[:, t], every(levels[:, k, :], GH), ALU.mult))
                v.feed()
                four(lambda t, b: cp(T1[:, t], b))
                v.feed()
                if k < LEVELS - 1:
                    four(lambda t, b: tt(X[:, t], X[:, t], b, ALU.subtract))
                four(lambda t, b: tt(XT[:, t], XT[:, t], b, ALU.subtract))
            v.feed()
            four(lambda t, b: cp(u[:, t], b))
            four(lambda t, b: cp(wT[:, t], b))
            for n in range(S // CH):
                t, r0 = n // 2, CH * (n % 2)
                r = slice(r0, r0 + CH)
                if n:
                    v.feed()
                    b = v.q.take()
                    do(tt(u[r, t], u[r, t], view(ps[b], 0, (GH, P))[r], ALU.subtract), psum_free)
                v.feed()
                b = v.q.take()
                do(cp(o[r, t], view(ps[b], 0, (GH, P))[r]), psum_free)
                if n == 0:
                    b = v.q.take()
                    do(cp(state, view(ps[b], 0, (GH, P))), psum_free)
                elif n < S // CH - 1:
                    do(tt(state, state, along(eEnd[:, t, n % 2, :], P), ALU.mult))
                    b = v.q.take()
                    do(tt(state, state, view(ps[b], 0, (GH, P)), ALU.add), psum_free)
            do(tt(sq, o, o, ALU.mult))
            do(e.tensor_reduce(oss, sq, AX.X, ALU.add))
            v.ask()
            v.answer()
            do(e.reciprocal(orr, oss))
            for t in range(T):
                do(tt(o[:, t], o[:, t], along(orr[:, t], P), ALU.mult))
                do(tt(o[:, t], o[:, t], every(ogain[:], GH), ALU.mult))
                do(tt(mix[:, t, 512:1024].rearrange("p (h d) -> p h d", h=GH), o[:, t],
                      gz[:, t].rearrange("p (h d) -> p h d", h=GH), ALU.mult))
            v.feed()
            vec_to_features(v, xT, DC)
            vec_product_residual(v, 1.0)

        def act_part(a):
            f, do = a.eng.activation, a.do
            act_norm(a, h)
            a.get()
            do(f(beta, raw[:, :, 8:12], ACT.Sigmoid))
            do(f(lsp, neg, ACT.Exp))
            do(f(lsp, lsp, ACT.Ln, bias=1.0))
            do(f(ea, a_log, ACT.Exp))
            a.put()
            a.get()
            do(f(eG, G, ACT.Exp))
            do(f(eT, eT, ACT.Exp))
            a.put()
            a.get()
            do(f(conv, conv, ACT.Silu))
            do(f(gz, gz, ACT.Silu))
            a.put()
            a.get()
            for t in range(T):
                for hd in range(FH):
                    do(f(tiles[t][:, hd, :], tiles[t][:, hd, :], ACT.Exp,
                         bias=mx[:, t, hd:hd + 1], accum_out=den[:, t, hd:hd + 1]))
                a.put()
            a.get()
            for t in range(T):
                for hd in range(GH):
                    do(f(dec[:, t, hd, :], dec[:, t, hd, :], ACT.Exp, bias=nG[:, t, hd:hd + 1]))
            do(f(eEnd, eEnd, ACT.Exp))
            a.put()
            a.get()
            do(f(ss, ss, ACT.Sqrt, bias=eps[:]))
            a.put()
            a.get()
            do(f(oss, oss, ACT.Sqrt, bias=eps[:], scale=1.0 / GD))
            a.put()
            act_product_norm(a)

        def sp_part(sp):
            ff = by_feature("w_in", FF0, FH)
            gba = by_feature("w_in", GB0, 8)
            sp.load(lambda s: [(wide[s][:, :, 0:8], ff), (wide[s][:, 0:4, 8:16], gba[:, 0:4, :]),
                               (wide[s][:, 4:8, 8:16], gba[:, 4:8, :])])
            for lo in (GQ0, GQ0 + 512, GQ0 + 1024, 0, FK0, FV0, GZ0):
                sp.project("w_in", lo)
            for lo in (0, 512):
                sp.project("w_out", lo)
        return pe_part, vec_part, act_part, sp_part
    STAGE_PARTS["B"] = mixer()

    def memory():
        MH, HC = 4, 2
        memory_rows, e = carve(0, T, D)
        memT, e = carve(e, DC, S)
        kT, e = carve(e, DC, S)
        val, e = carve(e, T, D)
        qT, e = carve(e, DC, S)
        soft, e = carve(e, T, MH, S)
        softT, e = carve(e, MH, T, S)
        oT = memT
        mx, den = view(sm, 0, (T, MH)), view(sm, 8, (T, MH))
        mem_loaded = sem("mem_loaded")

        def pe_part(pe):
            mm, tr = pe.eng.matmul, pe.eng.transpose
            pe.get()
            pe_to_features(pe, strided(xn), DC)
            pe.get()
            for _ in range(2):
                pe_features(pe, memT)
            for _ in range(2):
                pe_tokens(pe, memT)
            pe.get()
            pe_to_features(pe, strided(xn), DC)
            pe.get()
            for _ in range(2):
                pe_features(pe, xT)
            pe.get()
            for t in range(T):
                for hd in range(0, MH, 2):
                    b = pe.q.fill()
                    for k in range(2):
                        for c in range(HC):
                            at = (hd + k) * HC + c
                            ins = mm(ps[b][:, k * S:(k + 1) * S], qT[:, at, t * P:(t + 1) * P],
                                     kT[:, at, :], start=c == 0, stop=c == HC - 1)
                    ins.then_inc(psum_full, 1)
            for t in range(T):
                pe.get()
                for hd in range(0, MH, 2):
                    b = pe.q.fill()
                    for k in range(2):
                        for m in range(T):
                            n = k * T + m
                            ins = tr(ps[b][:, n * P:(n + 1) * P],
                                     soft[:, t, hd + k, m * P:(m + 1) * P], ident[:])
                    ins.then_inc(psum_full, 1)
            pe.get()
            for c in range(0, DC, 2):
                b = pe.q.fill()
                for k in range(2):
                    for m in range(T):
                        ins = mm(ps[b][:, k * S:(k + 1) * S],
                                 val[:, m, (c + k) * P:(c + k + 1) * P],
                                 softT[:, (c + k) // HC, m, :], start=m == 0, stop=m == T - 1)
                ins.then_inc(psum_full, 1)
            pe.get()
            pe_product(pe, oT)

        def vec_part(v):
            e, do = v.eng, v.do
            v.eng.wait_ge(mem_loaded, 16)
            vec_norm(v, memory_rows)
            v.feed()
            vec_to_features(v, memT, DC, preg[:, 3])

            def take(dst, n):
                for c in range(0, DC, 2):
                    b = v.q.take()
                    do(e.tensor_copy(dst[:, c:c + 2, :], view(ps[b], 0, (2, S))), psum_free)

            take(kT, 4)
            for n in range(2):
                for t in range(T):
                    b = v.q.take()
                    do(e.tensor_copy(val[:, t, n * 512:(n + 1) * 512], ps[b][:]), psum_free)
            vec_norm(v, h)
            v.feed()
            vec_to_features(v, xT, DC, preg[:, 2])
            take(qT, 4)
            v.feed()
            scale = (MH / D) ** 0.5
            for t in range(T):
                for hd in range(0, MH, 2):
                    b = v.q.take()
                    do(e.tensor_scalar(soft[:, t, hd:hd + 2, :], view(ps[b], 0, (2, S)), scale,
                                       None, ALU.mult), psum_free)
            do(e.tensor_reduce(mx, soft, AX.X, ALU.max))
            do(e.tensor_scalar(mx, mx, -1.0, None, ALU.mult))
            v.ask()
            for t in range(T):
                v.answer()
                do(e.reciprocal(den[:, t], den[:, t]))
                do(e.tensor_tensor(soft[:, t], soft[:, t], along(den[:, t], S), ALU.mult))
                v.feed()
            for t in range(T):
                for hd in range(0, MH, 2):
                    b = v.q.take()
                    do(e.tensor_copy(
                        softT[:, hd:hd + 2, :, t * P:(t + 1) * P].rearrange(
                            "p h m q -> p (h m) q"), view(ps[b], 0, (4, P))), psum_free)
            v.feed()
            take(oT, 4)
            v.feed()
            vec_product_residual(v, 1.0)

        def act_part(a):
            act_norm(a, memory_rows)
            act_norm(a, h)
            a.get()
            for t in range(T):
                for hd in range(MH):
                    a.do(a.eng.activation(soft[:, t, hd, :], soft[:, t, hd, :], ACT.Exp,
                                          bias=mx[:, t, hd:hd + 1],
                                          accum_out=den[:, t, hd:hd + 1]))
                a.put()
            act_product_norm(a)

        def sp_part(sp):
            if sp.block:
                sp.eng.wait_ge(*release[sp.block - 1])
            sp.eng.dma_start(memory_rows, A["mem"].rearrange("b (t p) d -> p (b t) d", p=P))\
                  .then_inc(mem_loaded, 16)
            for lo in (0, 512):
                sp.project("mem_w_kv", lo)
            for lo in (1024, 1536):
                sp.project("mem_w_kv", lo)
            for lo in (0, 512):
                sp.project("mem_w_q", lo)
            for lo in (0, 512):
                sp.project("mem_w_o", lo, natural=True)
        return pe_part, vec_part, act_part, sp_part

    STAGE_PARTS["C"] = memory()

    SHIFT1, SCALE1, GATE1, SHIFT2, SCALE2, GATE2 = range(6)
    cT = sb("cT", [P, DC])
    BIAS0 = ARENA - D
    bias_rows, _ = carve(BIAS0, D)
    bias_loaded = sem("bias_rows_loaded")
    arena_free = sem("stage_E_left_arena")
    if "E" in STAGES or "F" in STAGES:
        params.append((cT[:], A["c_2"][0].rearrange("(p c) -> p c", c=DC)))

    def pe_mod(pe, which):
        for n in range(2):
            w = wide[pe.slot()]
            b = pe.q.fill()
            for c in range(DC):
                pe.eng.matmul(ps[b][:], cT[:, c:c + 1].to_broadcast([P, P]), w[:, c, :],
                              start=c == 0, stop=False)
            pe.eng.matmul(ps[b][:], ident[:, which:which + 1].to_broadcast([P, P]),
                          bias_rows[:, n * 512:(n + 1) * 512], start=False, stop=True)\
                  .then_inc(psum_full, 1)
            pe.released()

    def sp_mod(sp, which):
        for n in range(2):
            sp.project("w_ada_2", which * D + n * 512)

    def vec_mod(v, dst):
        for n in range(2):
            b = v.q.take()
            v.do(v.eng.tensor_copy(dst[:, n * 512:(n + 1) * 512], ps[b][:]), psum_free)

    def vec_ada_norm(v, scale, shift):
        g = v.gain()
        for n in range(2):
            at = slice(n * 512, (n + 1) * 512)
            b = v.q.take()
            v.do(v.eng.scalar_tensor_tensor(scale[:, at], ps[b][:], 1.0, g[:, at],
                                            ALU.add, ALU.mult), psum_free)
        vec_mod(v, shift)
        v.eng.sem_inc(gain_used, 1)
        vec_norm(v, h)
        for t in range(T):
            v.do(v.eng.tensor_tensor(xn[:, t], xn[:, t], scale, ALU.mult))
            v.do(v.eng.tensor_tensor(xn[:, t], xn[:, t], shift, ALU.add))
        v.feed()

    def vec_gated_product(v, banks, gate):
        for t in range(T):
            for n in range(2):
                at = slice(n * 512, (n + 1) * 512)
                v.do(v.eng.tensor_tensor(xn[:, t, at], banks(t, n)[:], gate[:, at], ALU.mult))
        v.do(v.eng.tensor_tensor(h[:], h[:], xn[:], ALU.add))

    def hybrid():
        TAPS, MAPS, HD, HEADS = 31, 16, 64, 8
        LAMBDA0 = 0.8 - 0.6 * math.exp(0.0)
        u, e = carve(0, DC, TAPS - 1 + S)
        acc, e = carve(e, DC, S)
        qk0 = e
        qk, e = carve(e, 2 * T, MAPS, HD)
        val, e = carve(e, T, D)
        qk_T0 = e
        qT, e = carve(e, HEADS, S)
        kT, e = carve(e, HEADS, S)
        assert e <= BIAS0
        sq = view(arena, qk_T0, (2 * T, MAPS, HD))
        rot_a, rot_b = (view(arena, qk_T0 + i * 512, (2 * T, MAPS, 8)) for i in range(2))
        tap_rows = arena[0:TAPS + 3, qk0 + 2048:qk0 + 2048 + D]
        soft, e = carve(0, MAPS * 3 * P)
        tiles = [soft[:, 0:MAPS * P].rearrange("p (m k) -> p m k", m=MAPS),
                 soft[:, MAPS * P:].rearrange("p (m k) -> p m k", m=MAPS)]
        softT, e = carve(e, 2 * HEADS, P)
        y_attn = qT.rearrange("p c s -> p (c s)").rearrange("p (t n) -> p t n", t=T)
        gate_conv = kT.rearrange("p c s -> p (c s)").rearrange("p (t n) -> p t n", t=T)
        gate_attn, e = carve(0, T, D)
        gate1, e = carve(e, D)
        scale1, shift1 = view(arena, 0, (D,)), view(arena, D, (D,))
        convT = xn

        ROWS = TAPS + 3
        taps = view(sm, 0, (DC, ROWS))
        f32s = lambda lo, *shape: view(sm, DC * ROWS + lo, shape)
        ss, mx, den = f32s(0, 2 * T, MAPS), f32s(64, T, MAPS), f32s(96, T, MAPS)
        ang, trig, turns = f32s(128, 2, T, 8), f32s(160, 2, T, 8), f32s(192, 2, T, 8)
        pos, lam, mean = f32s(224, T), f32s(226, 4), f32s(230, T)
        var, oss = f32s(232, T), f32s(236, T, HEADS)
        params_E = sb("hybrid_params", [P, 8 * HD + 8])
        pv = lambda lo, n: params_E[:, lo:lo + n]
        dw_b, ln_g, ln_b = (taps[:, :, TAPS + i] for i in range(3))
        qg, kg, lams, sub_g = pv(0, 64), pv(64, 64), pv(128, 256), pv(384, 128)
        inv_freq = pv(512, 8)
        pos_i = sb("positions", [P, T], I32)
        params.extend([(qg, A["q_norm_g_2"][0].partition_broadcast(P)),
                       (kg, A["k_norm_g_2"][0].partition_broadcast(P)),
                       (sub_g, A["subln_g_2"][0].partition_broadcast(P)),
                       (pos_i[:], A["positions_2"][0].rearrange("(t p) -> p t", p=P))])
        params.extend((lams[:, i * HD:(i + 1) * HD], A[n][0].partition_broadcast(P))
                      for i, n in enumerate(("lambda_q1_2", "lambda_k1_2", "lambda_q2_2",
                                             "lambda_k2_2")))
        taps_loaded = sem("tap_rows_loaded")
        conv_step = sem("conv_step")
        THETA, ROT = 500000.0, 16

        def pool_part(eng, g, gains_before):
            if gains_before:
                eng.wait_ge(gain_used, gains_before)
            g(eng.memset(bias_rows, 0.0))
            eng.dma_start(bias_rows[0:6], A["b_ada_2"].rearrange("l (j n) -> (l j) n", j=6))\
               .then_inc(bias_loaded, 16)
            eng.dma_start(bias_rows[6:7], A["b_pw2_2"]).then_inc(bias_loaded, 16)
            eng.dma_start(tap_rows[0:TAPS], A["conv_dw_2"][0]).then_inc(taps_loaded, 16)
            for i, name in enumerate(("conv_dw_b_2", "conv_ln_g_2", "conv_ln_b_2")):
                eng.dma_start(tap_rows[TAPS + i:TAPS + i + 1], A[name]).then_inc(taps_loaded, 16)

        def pe_part(pe):
            mm, tr = pe.eng.matmul, pe.eng.transpose
            pe.get()
            pe.eng.wait_ge(bias_loaded, 32)
            pe_mod(pe, SCALE1)
            pe_mod(pe, SHIFT1)
            pe.get()
            pe_to_features(pe, strided(xn), DC)
            pe.eng.wait_ge(taps_loaded, 64)
            b = pe.q.fill()
            for c in range(DC):
                ins = tr(ps[b][:, c * ROWS:(c + 1) * ROWS], tap_rows[:, c * P:(c + 1) * P],
                         ident[0:ROWS, 0:ROWS])
            ins.then_inc(psum_full, 1)
            pe.get()
            for _ in range(4):
                pe_features(pe, xT)
            for _ in range(6):
                pe_tokens(pe, xT)
            pe.get()
            for t in range(T):
                for c in range(0, DC, 4):
                    b = pe.q.fill()
                    for k in range(4):
                        ins = tr(ps[b][:, k * P:(k + 1) * P], acc[:, c + k, t * P:(t + 1) * P],
                                 ident[:])
                    ins.then_inc(psum_full, 1)
            pe.get()
            for i in range(2):
                pe_to_features(pe, lambda c, t: qk[:, i * T + t].rearrange(
                    "p m d -> p (m d)")[:, c * P:(c + 1) * P], HEADS)
            pe.get()
            pe_to_features(pe, lambda c, t: convT[:, t, c * P:(c + 1) * P], DC)
            pe.get()
            for n in range(2):
                pe_tokens(pe, acc, bias=(ident[:, 6:7].to_broadcast([P, P]),
                                         bias_rows[:, n * 512:(n + 1) * 512]))
            for t in range(T):
                kw = (t + 1) * P
                for maps in bank_heads(t, MAPS):
                    b = pe.q.fill()
                    for k, m in enumerate(maps):
                        r = slice(HD * (m % 2), HD * (m % 2 + 1))
                        ins = mm(ps[b][:, k * kw:(k + 1) * kw],
                                 qT[r, m // 2, t * P:(t + 1) * P], kT[r, m // 2, 0:kw],
                                 start=True, stop=True)
                    ins.then_inc(psum_full, 1)
            for t in range(T):
                pe.get()
                blocks = [(hd, k) for hd in range(HEADS) for k in range(t + 1)]
                for i in range(0, len(blocks), 4):
                    b = pe.q.fill()
                    for n, (hd, k) in enumerate(blocks[i:i + 4]):
                        ins = tr(ps[b][:, n * P:(n + 1) * P],
                                 tiles[t][:, 2 * hd, k * P:(k + 1) * P], ident[:])
                    ins.then_inc(psum_full, 1)
                pe.get()
                for h0 in range(0, HEADS, 4):
                    b = pe.q.fill()
                    for n in range(4):
                        hd = h0 + n
                        for k in range(t + 1):
                            ins = mm(ps[b][:, n * P:(n + 1) * P], softT[:, (t + 1) * hd + k, :],
                                     val[:, k, hd * P:(hd + 1) * P], start=k == 0, stop=k == t)
                    ins.then_inc(psum_full, 1)
            for _ in range(4):
                pe_tokens(pe, xT)
            pe_mod(pe, GATE1)
            pe.get()
            pe_to_features(pe, strided(y_attn), DC)
            pe.get()
            pe_product(pe, xT)

        def vec_part(v):
            e, do = v.eng, v.do
            tt, ts, cp, stt = e.tensor_tensor, e.tensor_scalar, e.tensor_copy, \
                e.scalar_tensor_tensor
            v.ask()
            v.answer()
            v.feed()
            for i in range(8):
                f = float(np.float32(THETA) ** np.float32(-2.0 * i / ROT))
                do(e.memset(inv_freq[:, i:i + 1], f))
            do(cp(pos, pos_i[:]))
            for t in range(T):
                do(ts(ang[:, 0, t], inv_freq, pos[:, t:t + 1], None, ALU.mult))
            do(cp(ang[:, 1], ang[:, 0]))
            do(ts(turns[:, 0], ang[:, 0], 1.0 / (2 * math.pi), None, ALU.mult))
            do(ts(turns[:, 1], ang[:, 1], 1.0 / (2 * math.pi), 0.25, ALU.mult, ALU.add))
            do(ts(turns, turns, 1.5 * 2 ** 23, None, ALU.add))
            do(ts(turns, turns, -1.5 * 2 ** 23, None, ALU.add))
            left = 2 * math.pi
            for bits in (2.0 ** -5, 2.0 ** -15, None):
                part = float(np.float32(left)) if bits is None else round(left / bits) * bits
                left -= part
                do(stt(ang, turns, -part, ang, ALU.mult, ALU.add))
            do(ts(ang[:, 1], ang[:, 1], math.pi / 2, None, ALU.add))
            top = float(np.nextafter(np.float32(math.pi), np.float32(0)))
            do(ts(ang, ang, top, -top, ALU.min, ALU.max))
            for i in range(2):
                a_, b_ = (lams[:, (2 * i + j) * HD:(2 * i + j + 1) * HD] for j in range(2))
                do(tt(a_, a_, b_, ALU.mult))
                do(e.tensor_reduce(lam[:, i:i + 1], a_, AX.X, ALU.add))
            v.ask()
            v.answer()
            do(tt(lam[:, 2:3], lam[:, 1:2], lam[:, 0:1], ALU.subtract))
            do(ts(lam[:, 2:3], lam[:, 2:3], -LAMBDA0, None, ALU.add))
            vec_ada_norm(v, scale1, shift1)
            vec_to_features_only(v, xT, DC)
            b = v.q.take()
            do(cp(taps, view(ps[b], 0, (DC, ROWS))), psum_free)
            v.feed()
            do(e.memset(u[:, :, 0:TAPS - 1], 0.0))
            for c in range(0, DC, 2):
                b = v.q.take()
                do(cp(acc[:, c:c + 2, :], view(ps[b], 0, (2, S))), psum_free)
            for c in range(0, DC, 2):
                b = v.q.take()
                do(cp(u[:, c:c + 2, TAPS - 1:], view(ps[b], 0, (2, S))), psum_free)
            v.ask()
            v.answer()
            do(tt(u[:, :, TAPS - 1:], u[:, :, TAPS - 1:], acc, ALU.mult))

            steps = [(i, c) for i in range(TAPS) for c in range(DC)]
            done = [0]

            def convolve(n):
                for i, c in steps[done[0]:done[0] + n]:
                    src = u[:, c, i:i + S]
                    if i == 0:
                        ins = ts(acc[:, c, :], src, taps[:, c, 0:1], dw_b[:, c:c + 1],
                                 ALU.mult, ALU.add)
                    else:
                        e.wait_ge(conv_step, done[0] - DC + 1)
                        ins = stt(acc[:, c, :], src, taps[:, c, i:i + 1], acc[:, c, :],
                                  ALU.mult, ALU.add)
                    ins.then_inc(conv_step, 1)
                    done[0] += 1

            for i in range(3):
                for n in range(2):
                    for t in range(T):
                        b = v.q.take()
                        if i < 2:
                            dst = qk[:, i * T + t, n * 8:(n + 1) * 8, :]
                            do(cp(dst, view(ps[b], 0, (8, HD))), psum_free)
                        else:
                            do(cp(val[:, t, n * 512:(n + 1) * 512], ps[b][:]), psum_free)
                        convolve(21)
            assert done[0] == len(steps)
            e.wait_ge(conv_step, len(steps))
            v.feed()
            for t in range(T):
                for c in range(0, D, 512):
                    b = v.q.take()
                    do(cp(convT[:, t, c:c + 512], ps[b][:]), psum_free)
            do(tt(sq, qk, qk, ALU.mult))
            do(e.tensor_reduce(ss, sq, AX.X, ALU.add))
            do(e.tensor_reduce(mean, convT[:], AX.X, ALU.add))
            do(ts(mean, mean, 1.0 / D, None, ALU.mult))
            for t in range(T):
                do(ts(convT[:, t], convT[:, t], mean[:, t:t + 1], None, ALU.subtract))
            v.ask()
            v.answer()
            do(e.reciprocal(ss, ss))
            for i in range(2 * T):
                x = qk[:, i]
                do(tt(x, x, along(ss[:, i], HD), ALU.mult))
                do(tt(x, x, every(qg if i < T else kg, MAPS), ALU.mult))
                sin, cos = (every(trig[:, j, i % T], MAPS) for j in range(2))
                x1, x2 = x[:, :, 0:8], x[:, :, 8:16]
                do(tt(rot_a[:, i], x1, sin, ALU.mult))
                do(tt(rot_b[:, i], x2, sin, ALU.mult))
                do(tt(x1, x1, cos, ALU.mult))
                do(tt(x2, x2, cos, ALU.mult))
                do(tt(x1, x1, rot_b[:, i], ALU.subtract))
                do(tt(x2, x2, rot_a[:, i], ALU.add))
            v.feed()
            do(e.reciprocal(var, var))
            for t in range(T):
                do(ts(convT[:, t], convT[:, t], var[:, t:t + 1], None, ALU.mult))
            vec_to_features_only(v, qT, HEADS)
            vec_to_features_only(v, kT, HEADS)
            v.feed()
            for c in range(0, DC, 2):
                v.hand()
            v.ask()
            v.answer()
            v.give_back(4)
            v.feed()
            for n in range(2):
                for t in range(T):
                    b = v.q.take()
                    do(cp(convT[:, t, n * 512:(n + 1) * 512], ps[b][:]), psum_free)
            for t in range(T):
                kw = (t + 1) * P
                for maps in bank_heads(t, MAPS):
                    b = v.q.take()
                    m0 = maps[0]
                    do(cp(tiles[t][:, m0:maps[-1] + 1:2, :], view(ps[b], 0, (len(maps), kw))),
                       psum_free)
                diag = tiles[t][:, :, t * P:kw]
                do(tt(diag, diag, every(causal[:], MAPS), ALU.add))
                do(e.tensor_reduce(mx[:, t], tiles[t], AX.X, ALU.max))
                do(ts(mx[:, t], mx[:, t], -HD ** -0.5, None, ALU.mult))
                v.ask()
            for t in range(T):
                kw = (t + 1) * P
                v.answer()
                do(e.reciprocal(den[:, t], den[:, t]))
                do(ts(den[:, t, 1::2], den[:, t, 1::2], lam[:, 2:3], None, ALU.mult))
                do(tt(tiles[t], tiles[t], along(den[:, t], kw), ALU.mult))
                do(tt(tiles[t][:, 0::2, :], tiles[t][:, 0::2, :], tiles[t][:, 1::2, :], ALU.add))
                v.feed()
                for i in range(0, HEADS * (t + 1), 4):
                    b = v.q.take()
                    do(cp(softT[:, i:i + 4, :], view(ps[b], 0, (4, P))), psum_free)
                v.feed()
                for c in range(0, D, 512):
                    b = v.q.take()
                    do(cp(y_attn[:, t, c:c + 512], ps[b][:]), psum_free)
            for t in range(T):
                heads = y_attn[:, t].rearrange("p (h d) -> p h d", h=HEADS)
                scratch = gate_conv[:, t].rearrange("p (h d) -> p h d", h=HEADS)
                do(tt(scratch, heads, heads, ALU.mult))
                do(e.tensor_reduce(oss[:, t], scratch, AX.X, ALU.add))
            v.ask()
            v.answer()
            do(e.reciprocal(oss, oss))
            do(ts(oss, oss, 1.0 - LAMBDA0, None, ALU.mult))
            for t in range(T):
                heads = y_attn[:, t].rearrange("p (h d) -> p h d", h=HEADS)
                do(tt(heads, heads, along(oss[:, t], P), ALU.mult))
                do(tt(heads, heads, every(sub_g, HEADS), ALU.mult))
            for dst in (gate_conv, gate_attn):
                for n in range(2):
                    for t in range(T):
                        b = v.q.take()
                        do(cp(dst[:, t, n * 512:(n + 1) * 512], ps[b][:]), psum_free)
                v.ask()
            vec_mod(v, gate1)
            v.answer()
            v.answer()
            do(tt(convT[:], convT[:], gate_conv, ALU.mult))
            do(tt(y_attn, y_attn, gate_attn, ALU.mult))
            do(tt(y_attn, y_attn, convT[:], ALU.add))
            v.feed()
            vec_to_features_only(v, xT, DC)
            v.feed()
            got = [v.q.take() for _ in range(4)]
            vec_gated_product(v, lambda t, n: ps[got[2 * n + t]], gate1)
            v.give_back(4)
            e.sem_inc(arena_free, 1)

        def act_part(a):
            f, do = a.eng.activation, a.do
            a.get()
            do(f(cT[:], cT[:], ACT.Silu))
            a.put()
            a.get()
            do(f(lam[:, 0:2], lam[:, 0:2], ACT.Exp))
            do(f(trig, ang, ACT.Sin))
            a.put()
            act_norm(a, h)
            a.get()
            do(f(u[:, :, TAPS - 1:], u[:, :, TAPS - 1:], ACT.Sigmoid))
            a.put()
            a.get()
            do(f(ss, ss, ACT.Sqrt, bias=eps[:], scale=1.0 / HD))
            for t in range(T):
                do(f(gate_scratch[:], convT[:, t], ACT.Square, accum_out=var[:, t:t + 1]))
            do(f(var, var, ACT.Sqrt, bias=eps[:], scale=1.0 / D))
            a.put()
            a.get()
            for c in range(0, DC, 2):
                bank = a.bank()
                for k in range(2):
                    do(f(acc[:, c + k, :], bank[:, k * S:(k + 1) * S], ACT.Silu,
                         bias=ln_b[:, c + k:c + k + 1], scale=ln_g[:, c + k:c + k + 1]))
            a.put()
            for t in range(T):
                a.get()
                for m in range(MAPS):
                    do(f(tiles[t][:, m, :], tiles[t][:, m, :], ACT.Exp, scale=HD ** -0.5,
                         bias=mx[:, t, m:m + 1], accum_out=den[:, t, m:m + 1]))
                a.put()
            a.get()
            do(f(oss, oss, ACT.Sqrt, bias=eps[:], scale=1.0 / P))
            a.put()
            for dst in (gate_conv, gate_attn):
                a.get()
                do(f(dst, dst, ACT.Sigmoid))
                a.put()

        gate_scratch = view(arena, 0, (D,))

        def sp_part(sp):
            sp_mod(sp, SCALE1)
            sp_mod(sp, SHIFT1)
            for lo in range(0, 5 * D, 512):
                sp.project("w_in_2", lo)
            for lo in (0, 512):
                sp.project("w_pw2_2", lo, natural=True)
            for lo in range(5 * D, 7 * D, 512):
                sp.project("w_in_2", lo)
            sp_mod(sp, GATE1)
            for lo in (0, 512):
                sp.project("w_out_2", lo)
        return (pe_part, vec_part, act_part, sp_part), pool_part

    def vec_to_features_only(v, dst, chunks):
        for c in range(0, chunks, 2):
            b = v.q.take()
            v.do(v.eng.tensor_copy(dst[:, c:c + 2, :], view(ps[b], 0, (2, S))), psum_free)

    if "E" in STAGES:
        STAGE_PARTS["E"], pool_E = hybrid()

    def experts():
        GROUPS, PER, TOP_GROUPS, SCALE = 8, 8, 4, 2.5
        router, e = carve(ff_end, DC, N_EXP)
        gate2, e = carve(e, D)
        scale2, e = carve(e, D)
        shift2, e = carve(e, D)
        gates, e = carve(e, T, N_EXP)
        scores, e = carve(e, T, N_EXP)
        choice, e = carve(e, T, N_EXP)
        left, e = carve(e, T, N_EXP)
        best, e = carve(e, T, GROUPS, 8)
        more, e = carve(e, T, GROUPS, GROUPS)
        gatesT, e = carve(e, S)
        bias64, e = carve(e, N_EXP)
        assert e <= BIAS0
        gsum, rank, total = view(sm, 0, (T, GROUPS)), view(sm, 16, (T, GROUPS)), \
            view(sm, 32, (T,))
        router_loaded, gates_stored = sem("router_loaded"), sem("gates_stored")
        gate_loaded = [sem(f"gate_row_loaded{i}") for i in range(NS)]
        hidden_set = ff_sems("moe")[2]
        NB = N_EXP + 1

        def pool_part(eng, g, load_bias):
            if not load_bias:
                eng.wait_ge(arena_free, 1)
            if load_bias:
                g(eng.memset(bias_rows, 0.0))
                eng.dma_start(bias_rows[0:6], A["b_ada_2"].rearrange("l (j n) -> (l j) n", j=6))\
                   .then_inc(bias_loaded, 16)
                eng.dma_start(bias_rows[6:7], A["b_pw2_2"]).then_inc(bias_loaded, 16)
            eng.dma_start(router, weight("w_router_2").rearrange("(p c) n -> p c n", c=DC))\
               .then_inc(router_loaded, 16)
            eng.dma_start(bias64, A["router_bias_2"][0].partition_broadcast(P))\
               .then_inc(router_loaded, 16)
            eng.wait_ge(gates_stored, 16)

            def gate_row(x, slot):
                eng.dma_start(gate_rows[:, slot, :].unsqueeze(1),
                              gates_dram[bass.ds(x, 1), :].partition_broadcast(P))\
                   .then_inc(gate_loaded[slot], 16)

            for x in range(NS):
                gate_row(x, x)
            with eng.Fori(0, N_EXP // NS - 1) as j:
                for i in range(NS):
                    eng.wait_ge(hidden_set, 2 * (NS * j + i + 1) + 2)
                    gate_row(NS * j + NS + i, i)

        def pe_part(pe):
            mm, tr = pe.eng.matmul, pe.eng.transpose
            pe.get()
            pe.eng.wait_ge(bias_loaded, 32)
            pe_mod(pe, SCALE2)
            pe_mod(pe, SHIFT2)
            pe_mod(pe, GATE2)
            pe.get()
            pe_to_features(pe, strided(xn), DC)
            pe.get()
            pe.eng.wait_ge(router_loaded, 32)
            b = pe.q.fill()
            for t in range(T):
                for c in range(DC):
                    ins = mm(ps[b][:, t * N_EXP:(t + 1) * N_EXP], xT[:, c, t * P:(t + 1) * P],
                             router[:, c, :], start=c == 0, stop=c == DC - 1)
            ins.then_inc(psum_full, 1)
            pe.get()
            b = pe.q.fill()
            for t in range(T):
                ins = tr(ps[b][0:N_EXP, t * P:(t + 1) * P], gates[:, t, :], ident[:])
            ins.then_inc(psum_full, 1)
            pe_ff(pe, "moe", NB)

        def vec_part(v):
            e, do = v.eng, v.do
            tt, ts, cp = e.tensor_tensor, e.tensor_scalar, e.tensor_copy
            if "E" not in STAGES:
                v.ask()
                v.answer()
            v.feed()
            g = v.gain()
            for n in range(2):
                at = slice(n * 512, (n + 1) * 512)
                b = v.q.take()
                do(e.scalar_tensor_tensor(scale2[:, at], ps[b][:], 1.0, g[:, at],
                                          ALU.add, ALU.mult), psum_free)
            vec_mod(v, shift2)
            vec_mod(v, gate2)
            vec_norm(v, h)
            for t in range(T):
                do(tt(xn[:, t], xn[:, t], scale2, ALU.mult))
                do(tt(xn[:, t], xn[:, t], shift2, ALU.add))
            v.feed()
            vec_to_features(v, xT, DC)
            b = v.q.take()
            do(cp(left, view(ps[b], 0, (T, N_EXP))), psum_free)
            v.ask()
            v.answer()
            e.wait_ge(router_loaded, 32)
            do(tt(choice, scores, every(bias64, T), ALU.add))
            for t in range(T):
                for g_ in range(GROUPS):
                    do(e.max(best[:, t, g_, :], choice[:, t, g_ * PER:(g_ + 1) * PER]))
            do(tt(gsum, best[:, :, :, 0], best[:, :, :, 1], ALU.add))
            for t in range(T):
                mine, other = along(gsum[:, t], GROUPS), every(gsum[:, t], GROUPS)
                do(tt(more[:, t], other, mine, ALU.is_equal))
                do(tt(more[:, t], more[:, t], earlier[:], ALU.mult))
                do(tt(left[:, t].rearrange("p (a b) -> p a b", a=GROUPS), other, mine, ALU.is_gt))
                do(tt(more[:, t], more[:, t],
                      left[:, t].rearrange("p (a b) -> p a b", a=GROUPS), ALU.add))
            do(e.tensor_reduce(rank, more, AX.X, ALU.add))
            do(ts(rank, rank, TOP_GROUPS - 0.5, NEG, ALU.is_gt, ALU.mult))
            for t in range(T):
                by_group = choice[:, t].rearrange("p (g e) -> p g e", g=GROUPS)
                do(tt(by_group, by_group, along(rank[:, t], PER), ALU.add))
                do(e.max(best[:, t, 0, :], choice[:, t]))
                do(e.match_replace(left[:, t], best[:, t, 0, :], choice[:, t], 2 * NEG))
            do(tt(left, left, choice, ALU.not_equal))
            do(tt(gates, scores, left, ALU.mult))
            do(e.tensor_reduce(total, gates, AX.X, ALU.add))
            do(e.reciprocal(total, total))
            do(ts(total, total, SCALE, None, ALU.mult))
            do(tt(gates, gates, along(total, N_EXP), ALU.mult))
            v.feed()
            b = v.q.take()
            do(cp(gatesT[0:N_EXP], ps[b][0:N_EXP, 0:S]), psum_free)
            v.ask()
            vec_ff(v, "moe", NB, gate_loaded)
            vec_gated_product(v, ff_bank, gate2)

        def act_part(a):
            if "E" not in STAGES:
                a.get()
                a.do(a.eng.activation(cT[:], cT[:], ACT.Silu))
                a.put()
            act_norm(a, h)
            a.get()
            a.do(a.eng.activation(scores, left, ACT.Sigmoid))
            a.put()
            a.get()
            a.eng.dma_start(gates_dram, gatesT[0:N_EXP]).then_inc(gates_stored, 16)
            act_ff(a, "moe", NB)

        def sp_part(sp):
            sp_mod(sp, SCALE2)
            sp_mod(sp, SHIFT2)
            sp_mod(sp, GATE2)
            gu = A["w_exp_gu_2"].rearrange("l e (p c) n -> (l e) p c n", c=DC)
            dn = A["w_exp_down_2"].rearrange("l e (f p) n -> (l e) p f n", p=P)
            base = sp.block

            def parts(x):
                return lambda s: [
                    (wide[s][:, 0:4, :].unsqueeze(1),
                     gu[bass.ds(x, 1), :, 0:4, :].rearrange("e p c n -> p e c n")),
                    (wide[s][:, 4:8, :].unsqueeze(1),
                     gu[bass.ds(x, 1), :, 4:8, :].rearrange("e p c n -> p e c n")),
                    (down[s].unsqueeze(1), dn[bass.ds(x, 1)].rearrange("e p f n -> p e f n"))]

            sg = weight("w_sh_gu_2").rearrange("(p c) n -> p c n", c=DC)
            sd = weight("w_sh_down_2").rearrange("(f p) n -> p f n", p=P)
            sp.load(lambda s: [(wide[s][:, 0:4, :], sg[:, 0:4, :]),
                               (wide[s][:, 4:8, :], sg[:, 4:8, :]), (down[s], sd)])
            for b in range(1, NS):
                sp.load(parts(b - 1))
            down_done = ff_sems("moe")[3]
            with sp.eng.Fori(0, N_EXP // NS - 1) as j:
                for i in range(NS):
                    sp.eng.wait_ge(down_done, NS * j + i + 1)
                    s = (base + i) % NS
                    for dst, src in parts(NS * j + NS + i - 1)(s):
                        sp.eng.dma_start(dst, src).then_inc(loaded[s], 16)
            sp.block += N_EXP - NS
            sp.load(parts(N_EXP - 1))
        return (pe_part, vec_part, act_part, sp_part), pool_part

    if "F" in STAGES:
        STAGE_PARTS["F"], pool_F = experts()

    stages = [STAGE_PARTS[x] for x in STAGES]
    block = ctx.enter_context(nc.Block())

    @block.tensor
    def _(eng):
        pe = Pe(eng)
        eng.wait_ge(consts, 1)
        eng.wait_ge(params_loaded, 16 * len(params))
        for pe_part, _, _, _ in stages:
            pe_part(pe)

    @block.vector
    def _(eng):
        v = Vec(eng)
        eng.wait_ge(consts, 1)
        eng.wait_ge(params_loaded, 16 * len(params))
        eng.wait_ge(x_loaded, 16)
        for _, vec_part, _, _ in stages:
            vec_part(v)
        v.ask()

    @block.scalar
    def _(eng):
        a = Act(eng)
        eng.dma_start(h[:], A["x"].rearrange("b (t p) d -> p (b t) d", p=P)).then_inc(x_loaded, 16)
        for dst, src in params:
            eng.dma_start(dst, src, allow_slow_non_contiguous=True).then_inc(params_loaded, 16)
        eng.wait_ge(consts, 1)
        eng.wait_ge(params_loaded, 16 * len(params))
        for _, _, act_part, _ in stages:
            act_part(a)
        a.get()
        eng.dma_start(out.rearrange("b (t p) d -> p (b t) d", p=P), h[:]).then_inc(out_done, 16)
        eng.wait_ge(out_done, 16)

    @block.gpsimd
    def _(eng):
        g = Steps(eng, g_step)

        def select(ap, pattern, base, mult, op, fill):
            g(eng.affine_select(out=ap, in_=ap, pattern=pattern, compare_op=op, fill=fill,
                                base=base, channel_multiplier=mult))

        half = slice(0, P // 2)
        rest = slice(P // 2, P)
        g(eng.memset(eps[:], EPS))
        g(eng.memset(ident[:], 0.0))
        select(ident[:], [[-1, P]], 0, 1, ALU.not_equal, 1.0)
        g(eng.memset(tri1[:], 1.0))
        select(tri, [[1, P]], 0, -1, ALU.is_ge, 0.0)
        g(eng.memset(tri_chunk[:], 1.0))
        select(tri_chunk[:], [[1, P]], 0, -1, ALU.is_ge, 0.0)
        g(eng.memset(tri_chunk[half, rest], 0.0))
        g(eng.memset(ones_chunk[:], 0.0))
        g(eng.memset(ones_chunk[half, half], 1.0))
        g(eng.memset(ones_chunk[rest, rest], 1.0))
        g(eng.memset(causal[:], 0.0))
        select(causal[:], [[-1, P]], 0, 1, ALU.is_ge, NEG)
        g(eng.memset(causal_chunk[:], 0.0))
        select(causal_chunk[:], [[1, P]], 0, -1, ALU.is_ge, NEG)
        g(eng.memset(causal_chunk[half, rest], NEG))
        g(eng.memset(earlier[:], 1.0))
        select(earlier[:], [[1, 8], [-1, 8]], 0, 0, ALU.is_gt, 0.0)
        g(eng.memset(levels[:], 0.0))
        for k in range(LEVELS):
            w = 1 << k
            part = levels[:, k, :].rearrange("p (i c) -> p i c", c=2 * w)[:, :, w:2 * w]
            g(eng.memset(part, 1.0))
            select(part, [[-2 * w, P // (2 * w)], [0, w]], 0, 1, ALU.is_ge, 0.0)
            select(part, [[2 * w, P // (2 * w)], [0, w]], w, -1, ALU.is_gt, 0.0)
        eng.sem_inc(consts, 1)
        for k, name in enumerate(gain_order):
            if k >= 2:
                eng.wait_ge(gain_used, k - 1)
            eng.dma_start(gainb[k % 2][:], A[name][0].partition_broadcast(P))\
               .then_inc(gain_loaded[k % 2], 16)
        if "E" in STAGES:
            pool_E(eng, g, gain_order.index("norm1_g_2"))
        if "F" in STAGES:
            pool_F(eng, g, "E" not in STAGES)

    @block.sync
    def _(eng):
        sp = Sp(eng)
        for _, _, _, sp_part in stages:
            sp_part(sp)


def kernel(**inputs):
    import concourse.bacc as bacc
    from concourse.bass_utils import run_bass_kernel_spmd

    nc = bacc.Bacc("TRN2", target_bir_lowering=False, num_devices=1)
    arrays, aps = {}, {}
    for name, value in inputs.items():
        a = np.ascontiguousarray(value)
        arrays[f"in_{name}"] = a
        aps[name] = nc.dram_tensor(f"in_{name}", a.shape, mybir.dt.from_np(a.dtype),
                                   kind="ExternalInput").ap()
    out = nc.dram_tensor("out", inputs["x"].shape, F32, kind="ExternalOutput").ap()
    build(nc, aps, out)
    return run_bass_kernel_spmd(nc, [arrays], core_ids=[0]).results[0]["out"]
```

```python
from contextlib import ExitStack
import math

import numpy as np

import concourse.bass as bass
from concourse import mybir

F32 = mybir.dt.float32
F32R = mybir.dt.float32r
I32 = mybir.dt.int32
ALU = mybir.AluOpType
ACT = mybir.ActivationFunctionType
AX = mybir.AxisListType

P = 128
D = 1024
DC = D // P
S = 256
T = S // P
EPS = 1e-6
D_FF = 2816
FB = 256
NF = D_FF // FB
N_EXP = 64
NS = 4
SLOT = DC * 512 + 2 * D
LOADS = 3
PEEL = 2
STAGES = "ABCDEF"
NEG = -1e30
LEVELS = 6
ARENA = 16448


class Steps:

    def __init__(self, eng, own):
        self.eng, self.own, self.count = eng, own, {}

    def __call__(self, ins, sem=None):
        sem = self.own if sem is None else sem
        self.count[sem.name] = self.count.get(sem.name, 0) + 1
        ins.then_inc(sem, 1)
        self.eng.wait_ge(sem, self.count[sem.name])


class Queue:

    def __init__(self, eng, full, free):
        self.eng, self.full, self.free, self.n = eng, full, free, 0

    def fill(self):
        if self.n >= 8:
            self.eng.wait_ge(self.free, self.n - 7)
        self.n += 1
        return (self.n - 1) % 8

    def take(self):
        self.n += 1
        self.eng.wait_ge(self.full, self.n)
        return (self.n - 1) % 8

    def emptied(self):
        if self.n:
            self.eng.wait_ge(self.free, self.n)


def rounds(eng, n, peel):
    for a in range(min(peel, n)):
        yield a, 0
    loops = (n - peel) // NS
    if loops > 0:
        with eng.Fori(0, loops) as j:
            for u in range(NS):
                yield peel + u, j
    for a in range(peel + max(loops, 0) * NS, n):
        yield a, 0


def build(nc, A, out):
    with ExitStack() as ctx:
        program(nc, A, out, ctx)


def program(nc, A, out, ctx):
    sems = {}

    def sem(name):
        if name not in sems:
            sems[name] = ctx.enter_context(nc.semaphore(name))
        return sems[name]

    def sb(name, shape, dt=F32):
        return ctx.enter_context(nc.sbuf_tensor(name, shape, dt))

    ring = [sb(f"ring{i}", [P, SLOT]) for i in range(NS)]
    wide = [r[:, 0:DC * 512].rearrange("p (c n) -> p c n", c=DC) for r in ring]
    down = [r[:, DC * 512:SLOT].rearrange("p (f n) -> p f n", f=2) for r in ring]
    h = sb("h", [P, T, D])
    xn = sb("xn", [P, T, D])
    xT = sb("xT", [P, DC, S])
    ident = sb("ident", [P, P])
    tri1 = sb("tri1", [P, 2 * P])
    tri, ones = tri1[:, 0:P], tri1[:, P:2 * P]
    tri_chunk = sb("tri_chunk", [P, P])
    ones_chunk = sb("ones_chunk", [P, P])
    causal = sb("causal", [P, P])
    causal_chunk = sb("causal_chunk", [P, P])
    levels = sb("levels", [P, LEVELS, P])
    earlier = sb("earlier", [P, 8, 8])
    eps = sb("eps", [P, 1])
    stat = sb("stat", [P, 32])
    sm = sb("sm", [P, 528])
    gainb = [sb(f"gainb{i}", [P, D]) for i in range(2)]
    preg = sb("preg", [P, 5, DC])
    arena = sb("arena", [P, ARENA])
    ps = [ctx.enter_context(nc.psum_tensor(f"bank{i}", [P, 512], F32)) for i in range(8)]
    gates_dram = nc.dram_tensor("gates_by_expert", [N_EXP, S], F32).ap()
    hybrid_gates = nc.dram_tensor("hybrid_gates", [2, P, T, D], F32).ap()

    def view(t, start, shape):
        v = t[:, start:start + int(np.prod(shape))]
        names = "abcd"[:len(shape)]
        if len(shape) > 1:
            v = v.rearrange(f"p ({' '.join(names)}) -> p {' '.join(names)}",
                            **{k: s for k, s in zip(names, shape)})
        return v

    def carve(start, *shape):
        end = start + int(np.prod(shape))
        assert end <= ARENA, (start, shape)
        return view(arena, start, shape), end

    def every(ap, *shape):
        for _ in shape:
            ap = ap.unsqueeze(1)
        return ap.to_broadcast([ap.shape[0], *shape, ap.shape[-1]])

    def along(ap, n):
        ap = ap.unsqueeze(len(ap.shape))
        return ap.to_broadcast([*ap.shape[:-1], n])

    psum_full, psum_free = sem("psum_full"), sem("psum_free")
    loaded = [sem(f"slot_loaded{i}") for i in range(NS)]
    v_step, a_step, g_step = sem("vector_step"), sem("scalar_step"), sem("gpsimd_step")
    x_loaded, params_loaded, consts = sem("x_loaded"), sem("params_loaded"), sem("consts_made")
    operands_set = sem("operands_set")
    scalar_in = sem("scalar_input_set")
    scalar_out = sem("scalar_output_set")
    gain_loaded = [sem(f"gain_loaded{i}") for i in range(2)]
    gain_used = sem("gain_used")
    out_done = sem("out_done")

    release = []
    handed = []

    class Pe:
        def __init__(self, eng):
            self.eng, self.q = eng, Queue(eng, psum_full, psum_free)
            self.block = self.sets = 0

        def slot(self):
            b = self.block
            self.block += 1
            self.eng.wait_ge(loaded[b % NS], 16 * LOADS * (b // NS + 1))
            return b % NS

        def get(self):
            self.sets += 1
            self.eng.wait_ge(operands_set, self.sets)

        def released(self):
            release.append((psum_full, self.q.n))

    class Vec:
        def __init__(self, eng):
            self.eng, self.do = eng, Steps(eng, v_step)
            self.q = Queue(eng, psum_full, psum_free)
            self.outs = self.gains = 0

        def feed(self):
            self.eng.sem_inc(operands_set, 1)

        def ask(self):
            self.eng.sem_inc(scalar_in, 1)

        def answer(self):
            self.outs += 1
            self.eng.wait_ge(scalar_out, self.outs)

        def hand(self):
            b = self.q.take()
            handed.append(b)
            return b

        def give_back(self, n):
            self.eng.sem_inc(psum_free, n)
            self.do.count[psum_free.name] = self.do.count.get(psum_free.name, 0) + n

        def gain(self):
            k = self.gains
            self.gains += 1
            self.eng.wait_ge(gain_loaded[k % 2], 16 * (k // 2 + 1))
            return gainb[k % 2]

    class Act:
        def __init__(self, eng):
            self.eng, self.do = eng, Steps(eng, a_step)
            self.ins = self.hands = 0

        def get(self):
            self.ins += 1
            self.eng.wait_ge(scalar_in, self.ins)

        def put(self):
            self.eng.sem_inc(scalar_out, 1)

        def bank(self):
            self.hands += 1
            return ps[handed[self.hands - 1]]

    def act_norm(a, src):
        a.get()
        for t in range(T):
            a.do(a.eng.activation(xn[:, t], src[:, t], ACT.Square, accum_out=stat[:, t:t + 1]))
        a.do(a.eng.activation(stat[:, 2:4], stat[:, 0:2], ACT.Sqrt, bias=eps[:], scale=1.0 / D))
        a.put()

    def vec_norm(v, src):
        v.ask()
        v.answer()
        v.do(v.eng.reciprocal(stat[:, 4:6], stat[:, 2:4]))
        for t in range(T):
            v.do(v.eng.tensor_scalar(xn[:, t], src[:, t], stat[:, 4 + t:5 + t], None, ALU.mult))

    def act_bank_norm(a, banks):
        a.get()
        for t in range(T):
            for n in range(2):
                a.do(a.eng.activation(xn[:, t, n * 512:(n + 1) * 512], banks(t, n)[:],
                                      ACT.Square, accum_out=stat[:, 8 + 2 * n + t:9 + 2 * n + t]))
        for t in range(T):
            a.do(a.eng.activation(stat[:, 12 + t:13 + t], stat[:, 8 + t:9 + t],
                                  ACT.Identity, bias=stat[:, 10 + t:11 + t]))
        a.do(a.eng.activation(stat[:, 14:16], stat[:, 12:14], ACT.Sqrt, bias=eps[:],
                              scale=1.0 / D))
        a.put()

    def vec_residual(v, banks, weight):
        g = v.gain()
        v.ask()
        v.answer()
        v.do(v.eng.reciprocal(stat[:, 16:18], stat[:, 14:16]))
        v.do(v.eng.tensor_scalar(stat[:, 18:20], stat[:, 16:18], weight, None, ALU.mult))
        for t in range(T):
            for n in range(2):
                at = slice(n * 512, (n + 1) * 512)
                v.do(v.eng.scalar_tensor_tensor(xn[:, t, at], banks(t, n)[:],
                                                stat[:, 18 + t:19 + t], g[:, at],
                                                ALU.mult, ALU.mult))
        v.do(v.eng.tensor_tensor(h[:], h[:], xn[:], ALU.add))
        v.eng.sem_inc(gain_used, 1)

    def vec_to_features(v, dst, chunks, gain=None, tell=True):
        for c in range(0, chunks, 2):
            b = v.q.take()
            if gain is None:
                v.do(v.eng.tensor_copy(dst[:, c:c + 2, :], view(ps[b], 0, (2, S))), psum_free)
            else:
                for k in range(2):
                    v.do(v.eng.tensor_scalar(dst[:, c + k, :], ps[b][:, k * S:(k + 1) * S],
                                             gain[:, c + k:c + k + 1], None, ALU.mult),
                         psum_free if k else None)
        if tell:
            v.feed()

    def pe_to_features(pe, src, chunks):
        for c in range(0, chunks, 2):
            b = pe.q.fill()
            for k in range(2):
                for t in range(T):
                    ins = pe.eng.transpose(ps[b][:, k * S + t * P:k * S + (t + 1) * P],
                                           src(c + k, t), ident[:])
            ins.then_inc(psum_full, 1)

    def strided(src):
        v = src[:].rearrange("p t (q c) -> p t c q", c=DC)
        return lambda c, t: v[:, t, c, :]

    def pe_tokens(pe, lhs, n=512, bias=None):
        w = wide[pe.slot()]
        for t in range(T):
            b = pe.q.fill()
            for c in range(DC):
                ins = pe.eng.matmul(ps[b][:, 0:n], lhs[:, c, t * P:(t + 1) * P], w[:, c, 0:n],
                                    start=c == 0, stop=c == DC - 1 and bias is None)
            if bias is not None:
                ins = pe.eng.matmul(ps[b][:, 0:n], bias[0], bias[1], start=False, stop=True)
            ins.then_inc(psum_full, 1)
        pe.released()

    def pe_features(pe, rhs):
        w = wide[pe.slot()]
        for f in range(0, 4, 2):
            b = pe.q.fill()
            for k in range(2):
                for c in range(DC):
                    ins = pe.eng.matmul(ps[b][:, k * S:(k + 1) * S],
                                        w[:, c, (f + k) * P:(f + k + 1) * P], rhs[:, c, :],
                                        start=c == 0, stop=c == DC - 1)
            ins.then_inc(psum_full, 1)
        pe.released()

    def pe_product(pe, lhs):
        for _ in range(2):
            pe_tokens(pe, lhs)

    def vec_product_residual(v, weight):
        got = [v.hand() for _ in range(4)]
        vec_residual(v, lambda t, n: ps[got[2 * n + t]], weight)
        v.give_back(4)

    def act_product_norm(a):
        got = [a.bank() for _ in range(4)]
        act_bank_norm(a, lambda t, n: got[2 * n + t])

    def weight(name):
        w = A[name]
        return w.rearrange("l d n -> (l d) n") if len(w.shape) == 3 else w

    def by_feature(name, lo, n=512, natural=False):
        how = "(c p) n -> p c n" if natural else "(p c) n -> p c n"
        return weight(name).rearrange(how, c=DC)[:, :, lo:lo + n]

    class Sp:
        def __init__(self, eng):
            self.eng, self.block = eng, 0

        def load(self, parts):
            b = self.block
            self.block += 1
            if b >= NS:
                self.eng.wait_ge(*release[b - NS])
            pairs = parts(b % NS)
            assert len(pairs) == LOADS
            for dst, src in pairs:
                self.eng.dma_start(dst, src).then_inc(loaded[b % NS], 16)

        def project(self, name, lo, n=512, natural=False):
            src = by_feature(name, lo, n, natural)
            self.load(lambda s: [(wide[s][:, a:b, 0:n], src[:, a:b, :])
                                 for a, b in ((0, 3), (3, 6), (6, 8))])

    ff_sg, ff_end = carve(0, 2, S)
    ff_tmp, ff_end = carve(ff_end, 2, S)
    gate_rows, ff_end = carve(ff_end, NS, S)
    addr = {t: nc.lookup_mloc(x).addr for t, x in (("arena", arena), ("xn", xn), ("xT", xT))}

    def parts_at(name, where, start, *shape):
        return nc.alloc_sbuf_tensor_at(name, [P, *shape], F32R, offset=addr[where] + 4 * start)

    ff_h = [parts_at(f"hidden_{x}", "arena", ff_end + i * 4 * S, 2, 2, S)
            for i, x in enumerate(("high", "low"))]
    ff_end += 8 * S
    PIECE = 8 * S
    ff_w = [[parts_at(f"w{p}_{x}", "arena", ff_end + (2 * p + i) * PIECE,
                      *((DC, 2, P) if p < 2 else (2, D)))
             for i, x in enumerate(("high", "low"))] for p in range(3)]
    assert ff_end + 6 * PIECE <= ARENA
    x_high = parts_at("x_high", "xn", 0, DC, S)
    x_low = parts_at("x_low", "xT", 0, DC, S)
    PAIRS = ((0, 0), (0, 1), (1, 0))
    ff_bank = lambda t, n: ps[2 * t + n]

    def raw_piece(s, p):
        if p == 2:
            return down[s]
        return wide[s].rearrange("p c (k f n) -> p c k f n", k=2, f=2)[:, :, :, p, :]

    def ff_sems(tag):
        return [sem(f"{tag}_{x}") for x in ("gu_full", "silu_set", "hidden_set", "down_done")]

    def ff_weight_sems(tag):
        return [[sem(f"{tag}_{x}{p}") for p in range(3)] for x in ("high_set", "low_set")]

    def vec_cut_x(v):
        v.do(v.eng.tensor_copy(x_high[:], xT[:]))
        v.do(v.eng.tensor_tensor(x_low[:], xT[:], x_high[:].bitcast(F32), ALU.subtract))
        v.feed()

    def pe_ff(pe, tag, n):
        gu_full, _, hidden_set, down_done = ff_sems(tag)
        _, low_set = ff_weight_sems(tag)
        pe.get()
        pe.q.emptied()

        def second(a, j, first, last):
            b = a + NS * j
            pe.eng.wait_ge(hidden_set, 2 * b + 2)
            pe.eng.wait_ge(low_set[2], b + 1)
            for f in range(2):
                for t in range(T):
                    for i, (w, x) in enumerate(PAIRS):
                        for m in range(2):
                            ins = pe.eng.matmul(
                                ff_bank(t, m)[:], ff_h[x][:, a % 2, f, t * P:(t + 1) * P],
                                ff_w[2][w][:, f, m * 512:(m + 1) * 512],
                                start=first and f == 0 and i == 0,
                                stop=last and f == 1 and i == 2, skip_group_check=True)
            ins.then_inc(down_done, 1)

        for a, j in rounds(pe.eng, n, PEEL):
            b = a + NS * j
            if a >= PEEL:
                pe.eng.wait_ge(hidden_set, 2 * b - 2)
            for f in range(2):
                pe.eng.wait_ge(low_set[f], b + 1)
                bank = ps[4 + 2 * (a % 2) + f]
                for k in range(2):
                    for c in range(DC):
                        for i, (w, x) in enumerate(PAIRS):
                            ins = pe.eng.matmul(bank[:, k * S:(k + 1) * S],
                                                ff_w[f][w][:, c, k, :], (x_high, x_low)[x][:, c, :],
                                                start=c == 0 and i == 0,
                                                stop=c == DC - 1 and i == 2,
                                                skip_group_check=True)
                ins.then_inc(gu_full, 1)
            if a >= 1:
                second(a - 1, j, a == 1, False)
        second(n - 1, 0, False, True)
        release.extend((low_set[2], i + 1) for i in range(n))
        pe.block += n

    def act_ff(ac, tag, n, base):
        gu_full, silu_set, hidden_set, down_done = ff_sems(tag)
        high_set, _ = ff_weight_sems(tag)

        def cut(a, j, p):
            s = (base + a) % NS
            ac.eng.activation(ff_w[p][0][:], raw_piece(s, p), ACT.Copy).then_inc(high_set[p], 1)

        def arrived(a, j):
            ac.eng.wait_ge(loaded[(base + a) % NS], 16 * LOADS * ((base + a) // NS + 1 + j))

        ac.get()
        arrived(0, 0)
        cut(0, 0, 0)
        cut(0, 0, 1)
        for a, j in rounds(ac.eng, n, PEEL):
            b = a + NS * j
            more = a + 1 < n
            for f in range(2):
                ac.eng.wait_ge(gu_full, 2 * b + f + 1)
                if a >= 1:
                    ac.eng.wait_ge(hidden_set, 2 * b + f - 1)
                ac.eng.activation(ff_sg[:, f, :], ps[4 + 2 * (a % 2) + f][:, 0:S],
                                  ACT.Silu).then_inc(silu_set, 1)
                if more:
                    if f == 0:
                        arrived(a + 1, j)
                    cut(a + 1, j, f)
            if a >= 1:
                ac.eng.wait_ge(down_done, b)
            cut(a, j, 2)

    def vec_ff(v, tag, n, base, gate_loaded=None):
        _, silu_set, hidden_set, down_done = ff_sems(tag)
        high_set, low_set = ff_weight_sems(tag)
        hidden_step = sem(f"{tag}_hidden_step")
        v.ask()

        def cut(a, j, p):
            v.eng.wait_ge(high_set[p], a + NS * j + 1)
            v.eng.tensor_tensor(ff_w[p][1][:], raw_piece((base + a) % NS, p),
                                ff_w[p][0][:].bitcast(F32), ALU.subtract).then_inc(low_set[p], 1)

        cut(0, 0, 0)
        cut(0, 0, 1)
        for a, j in rounds(v.eng, n, PEEL):
            b = a + NS * j
            gated = gate_loaded is not None and a >= 1
            if a >= PEEL:
                v.eng.wait_ge(down_done, b - 1)
            if gated:
                v.eng.wait_ge(gate_loaded[(a - 1) % NS], 16 * ((a - 1) // NS + 1 + j))
            for f in range(2):
                steps = 2 * (2 * b + f) if gate_loaded is None else 3 * (2 * b + f) - 2
                if gate_loaded is not None and a == 0:
                    steps = 2 * f
                hid, (high, low) = ff_tmp[:, f, :], (x[:, a % 2, f, :] for x in ff_h)
                v.eng.wait_ge(silu_set, 2 * b + f + 1)
                v.eng.tensor_tensor(hid, ff_sg[:, f, :], ps[4 + 2 * (a % 2) + f][:, S:2 * S],
                                    ALU.mult).then_inc(hidden_step, 1)
                if gated:
                    v.eng.wait_ge(hidden_step, steps + 1)
                    v.eng.tensor_tensor(hid, hid, gate_rows[:, (a - 1) % NS, :],
                                        ALU.mult).then_inc(hidden_step, 1)
                    steps = steps + 1
                v.eng.wait_ge(hidden_step, steps + 1)
                v.eng.tensor_copy(high, hid).then_inc(hidden_step, 1)
                v.eng.wait_ge(hidden_step, steps + 2)
                v.eng.tensor_tensor(low, hid, high.bitcast(F32), ALU.subtract)\
                 .then_inc(hidden_set, 1)
                if a + 1 < n:
                    cut(a + 1, j, f)
            cut(a, j, 2)
        v.eng.wait_ge(down_done, n)

    def dense(tag, gain_at):
        base = []

        def pe_part(pe):
            pe.get()
            pe_to_features(pe, strided(xn), DC)
            base.append(pe.block)
            pe_ff(pe, tag, NF)

        def vec_part(v):
            vec_norm(v, h)
            v.feed()
            vec_to_features(v, xT, DC, preg[:, gain_at], False)
            vec_cut_x(v)
            vec_ff(v, tag, NF, base[0])
            vec_residual(v, ff_bank, 0.5)

        def act_part(a):
            act_norm(a, h)
            act_ff(a, tag, NF, base[0])
            act_bank_norm(a, ff_bank)

        def sp_part(sp):
            wg, wu = (weight(f"{tag}_w_{x}").rearrange("(p c) n -> p c n", c=DC)
                      for x in ("gate", "up"))
            wd = weight(f"{tag}_w_down").rearrange("(i f p) n -> i p f n", f=2, p=P)
            for i in range(NF):
                at = slice(i * FB, (i + 1) * FB)
                sp.load(lambda s: [(wide[s][:, :, 0:FB], wg[:, :, at]),
                                   (wide[s][:, :, FB:2 * FB], wu[:, :, at]),
                                   (down[s], wd[i])])
        return pe_part, vec_part, act_part, sp_part

    params = [(preg[:, i], A[n][0].rearrange("(p c) -> p c", c=DC)) for i, n in enumerate(
        ("ffn1_pre_norm", "mix_pre_norm", "mem_pre_norm", "mem_kv_norm", "ffn2_pre_norm"))]
    PRE_GAINS = len(params)
    gains_loaded = sem("pre_gains_loaded")
    gain_order = [n for s, n in zip("ABCDEF", (
        "ffn1_post_norm", "mix_post_norm", "mem_post_norm", "ffn2_post_norm", "norm1_g_2",
        "norm2_g_2")) if s in STAGES]

    STAGE_PARTS = {"A": dense("ffn1", 0), "D": dense("ffn2", 4)}

    FH, FD = 8, 64
    GH, GD, CH = 4, 128, 64
    PAD = 3
    FK0, FV0, FF0 = 512, 1024, 1536
    GQ0 = FF0 + FH
    GZ0, GB0 = GQ0 + 3 * 512, GQ0 + 4 * 512

    def bank_heads(t, heads):
        n = 4 // (t + 1)
        return [[2 * (i + k) + half for k in range(n)]
                for i in range(0, heads // 2, n) for half in range(2)]

    def mixer():
        qkvP, e = carve(0, 12, PAD + S)
        conv, e = carve(e, 12, S)
        qkv, e = carve(e, T, 12, P)
        gz, e = carve(e, T, 512)
        fox0 = e
        fqT, e = carve(e, 4, S)
        fkT, e = carve(e, 4, S)
        fv, e = carve(e, T, 512)
        Frow = xn[:].rearrange("p t (a s) -> p (t a) s", s=S)
        soft, e = carve(e, FH * 3 * P)
        tiles = [soft[:, 0:FH * P].rearrange("p (h k) -> p h k", h=FH),
                 soft[:, FH * P:3 * FH * P].rearrange("p (h k) -> p h k", h=FH)]
        softT, _ = carve(0, 3 * FH, P)
        qT, e = carve(0, GH, S)
        kT, e = carve(e, GH, S)
        kbT, e = carve(e, GH, S)
        qdT, e = carve(e, GH, S)
        dec, e = carve(e, T, GH, P)
        LT, e = carve(e, T, GH, P)
        kb, e = carve(fox0, T, GH, P)
        kbg, e = carve(e, T, GH, P)
        kt, e = carve(e, T, GH, P)
        qd, e = carve(e, T, GH, P)
        X, e = carve(e, T, GH, P)
        XT, e = carve(e, T, GH, P)
        Mb, T1 = qd, kb
        u, wT = Mb, T1
        state = kbT[:, 0:2, :].rearrange("p a (b d) -> p (a b) d", b=2)
        o = LT
        sq = X
        mix = xn

        def small(lo, *shape):
            return view(sm, lo, shape)

        raw, neg, lsp = small(0, T, 16), small(32, T, 16), small(64, T, 16)
        fg, ea, beta = small(96, T, 12), small(120, 4), small(124, T, GH)
        cum = small(132, 32)
        Fq, G, Gend = small(132, T, FH), small(148, T, GH), small(156, T, GH)
        nG, eG, eT = small(164, T, GH), small(172, T, GH), small(180, T, GH)
        eEnd = small(188, T, 2, GH)
        mx, den, rden = small(204, T, FH), small(220, T, FH), small(236, T, FH)
        ss, rr = small(252, T, 8), small(268, T, 8)
        cw = small(300, 4, 12)
        bias16, a_log = small(350, 16), small(366, 4)
        oss, orr = small(370, T, GH), small(378, T, GH)
        mix_conv_step = sem("mixer_conv_step")
        cw_rows = sb("gdn_tap_rows", [12, 4, P])
        ogain = sb("gdn_gain", [P, GD])

        params.extend([
            (bias16[:, 0:8], A["fox_f_bias"][0].partition_broadcast(P)),
            (bias16[:, 12:16], A["gdn_dt_bias"][0].partition_broadcast(P)),
            (a_log, A["gdn_a_log"][0].partition_broadcast(P)),
            (ogain[:], A["gdn_out_norm"][0].partition_broadcast(P)),
            (cw_rows[:], A["gdn_conv_w"][0].rearrange("i (c p) -> c i p", p=P)),
        ])

        def pe_part(pe):
            mm, tr = pe.eng.matmul, pe.eng.transpose
            pe.get()
            pe_to_features(pe, strided(xn), DC)
            pe.get()
            w = wide[pe.slot()]
            b = pe.q.fill()
            for t in range(T):
                for c in range(DC):
                    ins = mm(ps[b][:, t * 16:(t + 1) * 16], xT[:, c, t * P:(t + 1) * P],
                             w[:, c, 0:16], start=c == 0, stop=c == DC - 1)
            ins.then_inc(psum_full, 1)
            pe.released()
            b = pe.q.fill()
            for i in range(4):
                ins = tr(ps[b][:, 12 * i:12 * i + 12], cw_rows[:, i, :], ident[0:12, 0:12])
            ins.then_inc(psum_full, 1)
            for _ in range(5):
                pe_features(pe, xT)
            for _ in range(2):
                pe_tokens(pe, xT)
            pe.get()
            b = pe.q.fill()
            mm(ps[b][:, 0:8], tri, fg[:, 0, 0:8], start=True, stop=True)
            mm(ps[b][:, 8:16], tri, fg[:, 1, 0:8], start=True, stop=False)
            mm(ps[b][:, 8:16], ones, fg[:, 0, 0:8], start=False, stop=True)
            for t in range(T):
                mm(ps[b][:, 16 + 4 * t:20 + 4 * t], tri_chunk[:], fg[:, t, 8:12],
                   start=True, stop=True)
                ins = mm(ps[b][:, 24 + 4 * t:28 + 4 * t], ones_chunk[:], fg[:, t, 8:12],
                         start=True, stop=True)
            ins.then_inc(psum_full, 1)
            for hd in range(0, FH, 2):
                b = pe.q.fill()
                for k in range(2):
                    one = fg[:, 0, hd + k:hd + k + 1].to_broadcast([P, P])
                    two = fg[:, 1, hd + k:hd + k + 1].to_broadcast([P, P])
                    mm(ps[b][:, k * S:k * S + P], one, tri, start=True, stop=True)
                    mm(ps[b][:, k * S + P:(k + 1) * S], one, ones, start=True, stop=False)
                    ins = mm(ps[b][:, k * S + P:(k + 1) * S], two, tri, start=False, stop=True)
                ins.then_inc(psum_full, 1)
            for t in range(T):
                kw = (t + 1) * P
                for heads in bank_heads(t, FH):
                    b = pe.q.fill()
                    for k, hd in enumerate(heads):
                        r = slice(FD * (hd % 2), FD * (hd % 2 + 1))
                        ins = mm(ps[b][:, k * kw:(k + 1) * kw],
                                 fqT[r, hd // 2, t * P:(t + 1) * P], fkT[r, hd // 2, 0:kw],
                                 start=True, stop=True)
                    ins.then_inc(psum_full, 1)
            pe.get()
            for t in range(T):
                for c in range(0, 12, 4):
                    b = pe.q.fill()
                    for k in range(4):
                        ins = tr(ps[b][:, k * P:(k + 1) * P], conv[:, c + k, t * P:(t + 1) * P],
                                 ident[:])
                    ins.then_inc(psum_full, 1)
            for t in range(T):
                pe.get()
                blocks = [(hd, k) for hd in range(FH) for k in range(t + 1)]
                for i in range(0, len(blocks), 4):
                    b = pe.q.fill()
                    for n, (hd, k) in enumerate(blocks[i:i + 4]):
                        ins = tr(ps[b][:, n * P:(n + 1) * P], tiles[t][:, hd, k * P:(k + 1) * P],
                                 ident[:])
                    ins.then_inc(psum_full, 1)
            pe.get()
            for t in range(T):
                b = pe.q.fill()
                for hd in range(FH):
                    for k in range(t + 1):
                        at = hd if t == 0 else FH + 2 * hd + k
                        ins = mm(ps[b][:, hd * FD:(hd + 1) * FD], softT[:, at, :],
                                 fv[:, k, hd * FD:(hd + 1) * FD], start=k == 0, stop=k == t)
                ins.then_inc(psum_full, 1)
            for t in range(T):
                b = pe.q.fill()
                for hd in range(GH):
                    ins = mm(ps[b][:, hd * P:(hd + 1) * P],
                             fg[:, t, 8 + hd:9 + hd].to_broadcast([P, P]), tri_chunk[:],
                             start=True, stop=True)
                ins.then_inc(psum_full, 1)
            pe.get()
            for src in (qkv[:, :, 0:4, :], qkv[:, :, 4:8, :], kb, qd):
                for t in range(T):
                    b = pe.q.fill()
                    for hd in range(GH):
                        ins = tr(ps[b][:, hd * P:(hd + 1) * P], src[:, t, hd, :], ident[:])
                    ins.then_inc(psum_full, 1)
            pe.get()
            for rhs in (kbT, qT):
                for t in range(T):
                    b = pe.q.fill()
                    for hd in range(GH):
                        at = slice(t * P, (t + 1) * P)
                        ins = mm(ps[b][:, hd * P:(hd + 1) * P], kT[:, hd, at], rhs[:, hd, at],
                                 start=True, stop=True)
                    ins.then_inc(psum_full, 1)

            def four(lhs, rhs):
                for t in range(T):
                    b = pe.q.fill()
                    for hd in range(GH):
                        ins = mm(ps[b][:, hd * P:(hd + 1) * P], lhs[:, t, hd, :], rhs[:, t, hd, :],
                                 start=True, stop=True)
                    ins.then_inc(psum_full, 1)

            for k in range(LEVELS):
                pe.get()
                four(Mb, X)
                pe.get()
                if k < LEVELS - 1:
                    four(XT, T1)
                four(T1, XT)
            pe.get()
            four(XT, qkv[:, :, 8:12, :])
            four(kbg, XT)
            for n in range(S // CH):
                t, r0 = n // 2, CH * (n % 2)
                r = slice(r0, r0 + CH)
                at = slice(t * P + r0, t * P + r0 + CH)
                if n:
                    pe.get()
                    b = pe.q.fill()
                    for hd in range(GH):
                        ins = mm(ps[b][r, hd * P:(hd + 1) * P], wT[:, t, hd, r], state[:, hd, :],
                                 start=True, stop=True)
                    ins.then_inc(psum_full, 1)
                pe.get()
                b = pe.q.fill()
                for hd in range(GH):
                    if n:
                        mm(ps[b][r, hd * P:(hd + 1) * P], qdT[:, hd, at], state[:, hd, :],
                           start=True, stop=False)
                    ins = mm(ps[b][r, hd * P:(hd + 1) * P], dec[r, t, hd, r], u[r, t, hd, :],
                             start=n == 0, stop=True)
                ins.then_inc(psum_full, 1)
                if n < S // CH - 1:
                    b = pe.q.fill()
                    for hd in range(GH):
                        ins = mm(ps[b][:, hd * P:(hd + 1) * P], kt[r, t, hd, :], u[r, t, hd, :],
                                 start=True, stop=True)
                    ins.then_inc(psum_full, 1)
            pe.get()
            pe_to_features(pe, strided(mix), DC)
            MEM["pe_transposes"](pe)
            pe.get()
            pe_product(pe, xT)

        def vec_part(v):
            e, do = v.eng, v.do
            tt, ts, cp = e.tensor_tensor, e.tensor_scalar, e.tensor_copy
            do(e.memset(qkvP[:, :, 0:PAD], 0.0))
            do(e.memset(bias16[:, 8:12], 0.0))
            vec_norm(v, h)
            v.feed()
            vec_to_features(v, xT, DC, preg[:, 1])
            b = v.q.take()
            do(tt(raw, view(ps[b], 0, (T, 16)), every(bias16, T), ALU.add), psum_free)
            do(ts(neg, raw, -1.0, None, ALU.mult))
            do(tt(neg, raw, neg, ALU.min))
            v.ask()
            b = v.q.take()
            do(cp(cw, view(ps[b], 0, (4, 12))), psum_free)
            for c in range(0, 12, 2):
                b = v.q.take()
                do(cp(qkvP[:, c:c + 2, PAD:], view(ps[b], 0, (2, S))), psum_free)

            steps = [(i, c) for half in range(2) for i in range(4)
                     for c in range(6 * half, 6 * half + 6)]
            done = [0]

            def convolve():
                for i, c in steps[done[0]:done[0] + 6]:
                    if i == 0:
                        ins = ts(conv[:, c, :], qkvP[:, c, 0:S], cw[:, 0, c:c + 1], None, ALU.mult)
                    else:
                        e.wait_ge(mix_conv_step, done[0] - 5)
                        ins = e.scalar_tensor_tensor(conv[:, c, :], qkvP[:, c, i:i + S],
                                                     cw[:, i, c:c + 1], conv[:, c, :],
                                                     ALU.mult, ALU.add)
                    ins.then_inc(mix_conv_step, 1)
                    done[0] += 1

            for c in range(0, 4, 2):
                b = v.q.take()
                do(ts(fqT[:, c:c + 2, :], view(ps[b], 0, (2, S)), FD ** -0.5, None, ALU.mult),
                   psum_free)
                convolve()
            for c in range(0, 4, 2):
                b = v.q.take()
                do(cp(fkT[:, c:c + 2, :], view(ps[b], 0, (2, S))), psum_free)
                convolve()
            for dst in (fv, gz):
                for t in range(T):
                    b = v.q.take()
                    do(cp(dst[:, t, :], ps[b][:]), psum_free)
                    convolve()
            assert done[0] == len(steps)
            v.answer()
            do(ts(neg, raw, 0.0, None, ALU.min))
            do(tt(fg[:, :, 0:8], neg[:, :, 0:8], lsp[:, :, 0:8], ALU.subtract))
            do(ts(raw, raw, 0.0, None, ALU.max))
            do(tt(fg[:, :, 8:12], raw[:, :, 12:16], lsp[:, :, 12:16], ALU.add))
            do(ts(ea, ea, -1.0, None, ALU.mult))
            do(tt(fg[:, :, 8:12], fg[:, :, 8:12], every(ea, T), ALU.mult))
            v.feed()
            b = v.q.take()
            do(cp(cum, ps[b][:, 0:32]), psum_free)
            do(ts(nG, G, -1.0, None, ALU.mult))
            do(tt(eT, Gend, G, ALU.subtract))
            v.ask()
            for hd in range(0, FH, 2):
                b = v.q.take()
                do(cp(Frow[:, hd:hd + 2, :], view(ps[b], 0, (2, S))), psum_free)
            e.wait_ge(mix_conv_step, len(steps))
            v.ask()
            for t in range(T):
                kw = (t + 1) * P
                for heads in bank_heads(t, FH):
                    b = v.q.take()
                    for k, hd in enumerate(heads):
                        do(e.scalar_tensor_tensor(
                            tiles[t][:, hd, :], ps[b][:, k * kw:(k + 1) * kw],
                            Fq[:, t, hd:hd + 1], Frow[:, hd, 0:kw],
                            ALU.add, ALU.subtract), psum_free if hd == heads[-1] else None)
                diag = tiles[t][:, :, t * P:kw]
                do(tt(diag, diag, every(causal[:], FH), ALU.add))
                do(e.tensor_reduce(mx[:, t], tiles[t], AX.X, ALU.max))
            do(ts(mx, mx, -1.0, None, ALU.mult))
            v.answer()
            v.answer()
            v.feed()
            v.ask()
            for t in range(T):
                for c in range(0, 12, 4):
                    b = v.q.take()
                    do(cp(qkv[:, t, c:c + 4, :], view(ps[b], 0, (4, P))), psum_free)
            for t in range(T):
                v.answer()
                v.feed()
                for i in range(0, FH * (t + 1), 4):
                    b = v.q.take()
                    do(cp(softT[:, FH * t + i:FH * t + i + 4, :], view(ps[b], 0, (4, P))),
                       psum_free)
            v.feed()
            do(e.reciprocal(rden, den))
            for t in range(T):
                b = v.q.take()
                do(tt(mix[:, t, 0:512].rearrange("p (h d) -> p h d", h=FH),
                      view(ps[b], 0, (FH, FD)), along(rden[:, t, :], FD), ALU.mult), psum_free)
            for t in range(T):
                b = v.q.take()
                do(tt(dec[:, t], view(ps[b], 0, (GH, P)), every(causal_chunk[:], GH), ALU.add))
                for n in range(2):
                    do(cp(eEnd[:, t, n, :],
                          view(ps[b], 0, (GH, P))[:, :, CH * n + CH - 1]),
                       psum_free if n else None)
            v.ask()
            do(tt(X, qkv[:, :, 0:4, :], qkv[:, :, 0:4, :], ALU.mult))
            do(e.tensor_reduce(ss[:, :, 0:4], X, AX.X, ALU.add))
            do(tt(X, qkv[:, :, 4:8, :], qkv[:, :, 4:8, :], ALU.mult))
            do(e.tensor_reduce(ss[:, :, 4:8], X, AX.X, ALU.add))
            v.ask()
            v.answer()
            v.answer()
            do(e.reciprocal(rr, ss))
            do(ts(rr[:, :, 0:4], rr[:, :, 0:4], GD ** -0.5, None, ALU.mult))
            for t in range(T):
                do(tt(qkv[:, t, 0:8, :], qkv[:, t, 0:8, :], along(rr[:, t], P), ALU.mult))
                k_, v_ = qkv[:, t, 4:8, :], qkv[:, t, 8:12, :]
                do(tt(kb[:, t], k_, along(beta[:, t], P), ALU.mult))
                do(tt(kbg[:, t], kb[:, t], along(eG[:, t], P), ALU.mult))
                do(tt(kt[:, t], k_, along(eT[:, t], P), ALU.mult))
                do(tt(qd[:, t], qkv[:, t, 0:4, :], along(eG[:, t], P), ALU.mult))
                do(tt(v_, v_, along(beta[:, t], P), ALU.mult))
            v.feed()
            for dst in (qT, kT, kbT, qdT):
                for t in range(T):
                    b = v.q.take()
                    do(cp(dst[:, :, t * P:(t + 1) * P], view(ps[b], 0, (GH, P))), psum_free)
            v.feed()
            for dst in (LT, dec):
                for t in range(T):
                    b = v.q.take()
                    do(tt(dst[:, t], view(ps[b], 0, (GH, P)), dec[:, t], ALU.mult), psum_free)
            for t in range(T):
                do(cp(X[:, t], every(ident[:], GH)))
                do(cp(XT[:, t], every(ident[:], GH)))

            MEM["vec_squares"](v)

            def four(op):
                for t in range(T):
                    b = v.q.take()
                    do(op(t, view(ps[b], 0, (GH, P))), psum_free)

            for k in range(LEVELS):
                for t in range(T):
                    do(tt(Mb[:, t], LT[:, t], every(levels[:, k, :], GH), ALU.mult))
                v.feed()
                four(lambda t, b: cp(T1[:, t], b))
                v.feed()
                if k < LEVELS - 1:
                    four(lambda t, b: tt(X[:, t], X[:, t], b, ALU.subtract))
                four(lambda t, b: tt(XT[:, t], XT[:, t], b, ALU.subtract))
                if k == 1:
                    MEM["vec_scale"](v)
            v.answer()
            v.feed()
            four(lambda t, b: cp(u[:, t], b))
            four(lambda t, b: cp(wT[:, t], b))
            for n in range(S // CH):
                t, r0 = n // 2, CH * (n % 2)
                r = slice(r0, r0 + CH)
                if n:
                    v.feed()
                    b = v.q.take()
                    do(tt(u[r, t], u[r, t], view(ps[b], 0, (GH, P))[r], ALU.subtract), psum_free)
                v.feed()
                b = v.q.take()
                do(cp(o[r, t], view(ps[b], 0, (GH, P))[r]), psum_free)
                if n == 0:
                    b = v.q.take()
                    do(cp(state, view(ps[b], 0, (GH, P))), psum_free)
                elif n < S // CH - 1:
                    do(tt(state, state, along(eEnd[:, t, n % 2, :], P), ALU.mult))
                    b = v.q.take()
                    do(tt(state, state, view(ps[b], 0, (GH, P)), ALU.add), psum_free)
            do(tt(sq, o, o, ALU.mult))
            do(e.tensor_reduce(oss, sq, AX.X, ALU.add))
            v.ask()
            v.answer()
            do(e.reciprocal(orr, oss))
            for t in range(T):
                do(tt(o[:, t], o[:, t], along(orr[:, t], P), ALU.mult))
                do(tt(o[:, t], o[:, t], every(ogain[:], GH), ALU.mult))
                do(tt(mix[:, t, 512:1024].rearrange("p (h d) -> p h d", h=GH), o[:, t],
                      gz[:, t].rearrange("p (h d) -> p h d", h=GH), ALU.mult))
            v.feed()
            vec_to_features(v, xT, DC)
            MEM["vec_transposed"](v)
            vec_product_residual(v, 1.0)

        def act_part(a):
            f, do = a.eng.activation, a.do
            act_norm(a, h)
            a.get()
            do(f(beta, raw[:, :, 8:12], ACT.Sigmoid))
            do(f(lsp, neg, ACT.Exp))
            do(f(lsp, lsp, ACT.Ln, bias=1.0))
            do(f(ea, a_log, ACT.Exp))
            a.put()
            a.get()
            do(f(eG, G, ACT.Exp))
            do(f(eT, eT, ACT.Exp))
            a.put()
            a.get()
            do(f(conv, conv, ACT.Silu))
            do(f(gz, gz, ACT.Silu))
            a.put()
            a.get()
            for t in range(T):
                for hd in range(FH):
                    do(f(tiles[t][:, hd, :], tiles[t][:, hd, :], ACT.Exp,
                         bias=mx[:, t, hd:hd + 1], accum_out=den[:, t, hd:hd + 1]))
                a.put()
            a.get()
            for t in range(T):
                for hd in range(GH):
                    do(f(dec[:, t, hd, :], dec[:, t, hd, :], ACT.Exp, bias=nG[:, t, hd:hd + 1]))
            do(f(eEnd, eEnd, ACT.Exp))
            a.put()
            a.get()
            do(f(ss, ss, ACT.Sqrt, bias=eps[:]))
            a.put()
            MEM["act_squares"](a)
            MEM["act_scale"](a)
            a.get()
            do(f(oss, oss, ACT.Sqrt, bias=eps[:], scale=1.0 / GD))
            a.put()
            act_product_norm(a)

        def sp_part(sp):
            ff = by_feature("w_in", FF0, FH)
            gba = by_feature("w_in", GB0, 8)
            sp.load(lambda s: [(wide[s][:, :, 0:8], ff), (wide[s][:, 0:4, 8:16], gba[:, 0:4, :]),
                               (wide[s][:, 4:8, 8:16], gba[:, 4:8, :])])
            for lo in (GQ0, GQ0 + 512, GQ0 + 1024, 0, FK0, FV0, GZ0):
                sp.project("w_in", lo)
            MEM["sp_rows"](sp)
            for lo in (0, 512):
                sp.project("w_out", lo)
        return pe_part, vec_part, act_part, sp_part
    STAGE_PARTS["B"] = mixer()

    def memory():
        MH, HC = 4, 2
        memT, e = carve(0, DC, S)
        kT, e = carve(e, DC, S)
        val, e = carve(e, T, D)
        qT, e = carve(e, DC, S)
        soft, e = carve(e, T, MH, S)
        softT, e = carve(e, MH, T, S)
        oT = memT
        mx, den = view(sm, 0, (T, MH)), view(sm, 8, (T, MH))
        mem_block = []

        def mem_rows():
            flat = ring[mem_block[0] % NS][:]
            return view(flat, 0, (T, D)), view(flat, T * D, (T, D))

        def pe_transposes(pe):
            mem_block.append(pe.block)
            pe.slot()
            pe_to_features(pe, strided(mem_rows()[1]), DC)
            pe.released()

        def vec_squares(v):
            v.eng.wait_ge(loaded[mem_block[0] % NS], 16 * LOADS * (mem_block[0] // NS + 1))
            v.ask()

        def vec_scale(v):
            v.answer()
            v.do(v.eng.reciprocal(stat[:, 24:26], stat[:, 22:24]))
            v.ask()

        def act_squares(a):
            rows, normed = mem_rows()
            a.get()
            for t in range(T):
                a.do(a.eng.activation(normed[:, t], rows[:, t], ACT.Square,
                                      accum_out=stat[:, 20 + t:21 + t]))
            a.do(a.eng.activation(stat[:, 22:24], stat[:, 20:22], ACT.Sqrt, bias=eps[:],
                                  scale=1.0 / D))
            a.put()

        def act_scale(a):
            rows, normed = mem_rows()
            a.get()
            for t in range(T):
                a.do(a.eng.activation(normed[:, t], rows[:, t], ACT.Copy,
                                      scale=stat[:, 24 + t:25 + t]))
            a.put()

        def vec_transposed(v):
            vec_to_features(v, memT, DC, preg[:, 3])

        def sp_rows(sp):
            src = A["mem"].rearrange("b (t p) d -> p (b t) d", p=P)
            sp.load(lambda s: [(view(ring[s][:], 0, (T, D))[:, t, a:b], src[:, t, a:b])
                               for t, a, b in ((0, 0, D), (1, 0, 512), (1, 512, D))])

        def pe_part(pe):
            mm, tr = pe.eng.matmul, pe.eng.transpose
            pe.get()
            for _ in range(2):
                pe_features(pe, memT)
            for _ in range(2):
                pe_tokens(pe, memT)
            pe.get()
            pe_to_features(pe, strided(xn), DC)
            pe.get()
            for _ in range(2):
                pe_features(pe, xT)
            pe.get()
            for t in range(T):
                for hd in range(0, MH, 2):
                    b = pe.q.fill()
                    for k in range(2):
                        for c in range(HC):
                            at = (hd + k) * HC + c
                            ins = mm(ps[b][:, k * S:(k + 1) * S], qT[:, at, t * P:(t + 1) * P],
                                     kT[:, at, :], start=c == 0, stop=c == HC - 1)
                    ins.then_inc(psum_full, 1)
            for t in range(T):
                pe.get()
                for hd in range(0, MH, 2):
                    b = pe.q.fill()
                    for k in range(2):
                        for m in range(T):
                            n = k * T + m
                            ins = tr(ps[b][:, n * P:(n + 1) * P],
                                     soft[:, t, hd + k, m * P:(m + 1) * P], ident[:])
                    ins.then_inc(psum_full, 1)
            pe.get()
            for c in range(0, DC, 2):
                b = pe.q.fill()
                for k in range(2):
                    for m in range(T):
                        ins = mm(ps[b][:, k * S:(k + 1) * S],
                                 val[:, m, (c + k) * P:(c + k + 1) * P],
                                 softT[:, (c + k) // HC, m, :], start=m == 0, stop=m == T - 1)
                ins.then_inc(psum_full, 1)
            pe.get()
            pe_product(pe, oT)

        def vec_part(v):
            e, do = v.eng, v.do
            vec_norm(v, h)
            v.feed()

            def take(dst, n):
                for c in range(0, DC, 2):
                    b = v.q.take()
                    do(e.tensor_copy(dst[:, c:c + 2, :], view(ps[b], 0, (2, S))), psum_free)

            take(kT, 4)
            for n in range(2):
                for t in range(T):
                    b = v.q.take()
                    do(e.tensor_copy(val[:, t, n * 512:(n + 1) * 512], ps[b][:]), psum_free)
            vec_to_features(v, xT, DC, preg[:, 2])
            take(qT, 4)
            v.feed()
            scale = (MH / D) ** 0.5
            for t in range(T):
                for hd in range(0, MH, 2):
                    b = v.q.take()
                    do(e.tensor_scalar(soft[:, t, hd:hd + 2, :], view(ps[b], 0, (2, S)), scale,
                                       None, ALU.mult), psum_free)
            do(e.tensor_reduce(mx, soft, AX.X, ALU.max))
            do(e.tensor_scalar(mx, mx, -1.0, None, ALU.mult))
            v.ask()
            for t in range(T):
                v.answer()
                do(e.reciprocal(den[:, t], den[:, t]))
                do(e.tensor_tensor(soft[:, t], soft[:, t], along(den[:, t], S), ALU.mult))
                v.feed()
            for t in range(T):
                for hd in range(0, MH, 2):
                    b = v.q.take()
                    do(e.tensor_copy(
                        softT[:, hd:hd + 2, :, t * P:(t + 1) * P].rearrange(
                            "p h m q -> p (h m) q"), view(ps[b], 0, (4, P))), psum_free)
            v.feed()
            take(oT, 4)
            v.feed()
            vec_product_residual(v, 1.0)

        def act_part(a):
            act_norm(a, h)
            a.get()
            for t in range(T):
                for hd in range(MH):
                    a.do(a.eng.activation(soft[:, t, hd, :], soft[:, t, hd, :], ACT.Exp,
                                          bias=mx[:, t, hd:hd + 1],
                                          accum_out=den[:, t, hd:hd + 1]))
                a.put()
            act_product_norm(a)

        def sp_part(sp):
            for lo in (0, 512):
                sp.project("mem_w_kv", lo)
            for lo in (1024, 1536):
                sp.project("mem_w_kv", lo)
            for lo in (0, 512):
                sp.project("mem_w_q", lo)
            for lo in (0, 512):
                sp.project("mem_w_o", lo, natural=True)
        ahead = dict(pe_transposes=pe_transposes, vec_squares=vec_squares, vec_scale=vec_scale,
                     act_squares=act_squares, act_scale=act_scale, sp_rows=sp_rows,
                     vec_transposed=vec_transposed)
        return (pe_part, vec_part, act_part, sp_part), ahead

    STAGE_PARTS["C"], MEM = memory()

    SHIFT1, SCALE1, GATE1, SHIFT2, SCALE2, GATE2 = range(6)
    cT = sb("cT", [P, DC])
    BIAS0 = ARENA - D
    bias_rows, _ = carve(BIAS0, D)
    bias_loaded = sem("bias_rows_loaded")
    arena_free = sem("stage_E_left_arena")
    if "E" in STAGES or "F" in STAGES:
        params.append((cT[:], A["c_2"][0].rearrange("(p c) -> p c", c=DC)))

    def pe_mod(pe, which, halves=(0, 1)):
        for n in halves:
            w = wide[pe.slot()]
            b = pe.q.fill()
            for c in range(DC):
                pe.eng.matmul(ps[b][:], cT[:, c:c + 1].to_broadcast([P, P]), w[:, c, :],
                              start=c == 0, stop=False)
            pe.eng.matmul(ps[b][:], ident[:, which:which + 1].to_broadcast([P, P]),
                          bias_rows[:, n * 512:(n + 1) * 512], start=False, stop=True)\
                  .then_inc(psum_full, 1)
            pe.released()

    def sp_mod(sp, which):
        for n in range(2):
            sp.project("w_ada_2", which * D + n * 512)

    def vec_mod(v, dst):
        for n in range(2):
            b = v.q.take()
            v.do(v.eng.tensor_copy(dst[:, n * 512:(n + 1) * 512], ps[b][:]), psum_free)

    def vec_ada_norm(v, scale, shift):
        vec_norm(v, h)
        g = v.gain()
        for n in range(2):
            at = slice(n * 512, (n + 1) * 512)
            b = v.q.take()
            v.do(v.eng.scalar_tensor_tensor(scale[:, at], ps[b][:], 1.0, g[:, at],
                                            ALU.add, ALU.mult), psum_free)
        vec_mod(v, shift)
        v.eng.sem_inc(gain_used, 1)
        for t in range(T):
            v.do(v.eng.tensor_tensor(xn[:, t], xn[:, t], scale, ALU.mult))
            v.do(v.eng.tensor_tensor(xn[:, t], xn[:, t], shift, ALU.add))
        v.feed()

    def vec_gated_product(v, banks, gate):
        for t in range(T):
            for n in range(2):
                at = slice(n * 512, (n + 1) * 512)
                v.do(v.eng.tensor_tensor(xn[:, t, at], banks(t, n)[:], gate[:, at], ALU.mult))
        v.do(v.eng.tensor_tensor(h[:], h[:], xn[:], ALU.add))

    def hybrid():
        TAPS, MAPS, HD, HEADS = 31, 16, 64, 8
        LAMBDA0 = 0.8 - 0.6 * math.exp(0.0)
        u, e = carve(0, DC, TAPS - 1 + S)
        acc, e = carve(e, DC, S)
        qk0 = e
        qk, e = carve(e, 2 * T, MAPS, HD)
        val, e = carve(e, T, D)
        qk_T0 = e
        qT, e = carve(e, HEADS, S)
        kT, e = carve(e, HEADS, S)
        assert e <= BIAS0
        sq = view(arena, qk_T0, (2 * T, MAPS, HD))
        rot_a, rot_b = (view(arena, qk_T0 + i * 512, (2 * T, MAPS, 8)) for i in range(2))
        tap_rows = arena[0:TAPS + 3, qk0 + 2048:qk0 + 2048 + D]
        soft, e = carve(0, MAPS * 3 * P)
        tiles = [soft[:, 0:MAPS * P].rearrange("p (m k) -> p m k", m=MAPS),
                 soft[:, MAPS * P:].rearrange("p (m k) -> p m k", m=MAPS)]
        softT, e = carve(e, 2 * HEADS, P)
        y_attn = qT.rearrange("p c s -> p (c s)").rearrange("p (t n) -> p t n", t=T)
        gate_conv = kT.rearrange("p c s -> p (c s)").rearrange("p (t n) -> p t n", t=T)
        gate_attn = val
        gate_stage, e = carve(0, T, D)
        gate1, e = carve(e, D)
        gate_stored, gate_back = sem("hybrid_gate_stored"), sem("hybrid_gate_back")
        scale1, shift1 = view(arena, 0, (D,)), view(arena, D, (D,))
        convT = xn

        ROWS = TAPS + 3
        taps = view(sm, 0, (DC, ROWS))
        f32s = lambda lo, *shape: view(sm, DC * ROWS + lo, shape)
        ss, mx, den = f32s(0, 2 * T, MAPS), f32s(64, T, MAPS), f32s(96, T, MAPS)
        ang, trig, turns = f32s(128, 2, T, 8), f32s(160, 2, T, 8), f32s(192, 2, T, 8)
        pos, lam, mean = f32s(224, T), f32s(226, 4), f32s(230, T)
        var, oss = f32s(232, T), f32s(236, T, HEADS)
        params_E = sb("hybrid_params", [P, 8 * HD + 8])
        pv = lambda lo, n: params_E[:, lo:lo + n]
        dw_b, ln_g, ln_b = (taps[:, :, TAPS + i] for i in range(3))
        qg, kg, lams, sub_g = pv(0, 64), pv(64, 64), pv(128, 256), pv(384, 128)
        inv_freq = pv(512, 8)
        pos_i = sb("positions", [P, T], I32)
        params.extend([(qg, A["q_norm_g_2"][0].partition_broadcast(P)),
                       (kg, A["k_norm_g_2"][0].partition_broadcast(P)),
                       (sub_g, A["subln_g_2"][0].partition_broadcast(P)),
                       (pos_i[:], A["positions_2"][0].rearrange("(t p) -> p t", p=P))])
        params.extend((lams[:, i * HD:(i + 1) * HD], A[n][0].partition_broadcast(P))
                      for i, n in enumerate(("lambda_q1_2", "lambda_k1_2", "lambda_q2_2",
                                             "lambda_k2_2")))
        taps_loaded = sem("tap_rows_loaded")
        conv_step = sem("conv_step")
        THETA, ROT = 500000.0, 16

        def pool_part(eng, g, gains_before):
            if gains_before:
                eng.wait_ge(gain_used, gains_before)
            g(eng.memset(bias_rows, 0.0))
            eng.dma_start(bias_rows[0:6], A["b_ada_2"].rearrange("l (j n) -> (l j) n", j=6))\
               .then_inc(bias_loaded, 16)
            eng.dma_start(bias_rows[6:7], A["b_pw2_2"]).then_inc(bias_loaded, 16)
            eng.dma_start(tap_rows[0:TAPS], A["conv_dw_2"][0]).then_inc(taps_loaded, 16)
            for i, name in enumerate(("conv_dw_b_2", "conv_ln_g_2", "conv_ln_b_2")):
                eng.dma_start(tap_rows[TAPS + i:TAPS + i + 1], A[name]).then_inc(taps_loaded, 16)

        def pe_part(pe):
            mm, tr = pe.eng.matmul, pe.eng.transpose
            pe.get()
            pe.eng.wait_ge(bias_loaded, 32)
            pe_mod(pe, SCALE1)
            pe_mod(pe, SHIFT1)
            pe.get()
            pe_to_features(pe, strided(xn), DC)
            pe.eng.wait_ge(taps_loaded, 64)
            b = pe.q.fill()
            for c in range(DC):
                ins = tr(ps[b][:, c * ROWS:(c + 1) * ROWS], tap_rows[:, c * P:(c + 1) * P],
                         ident[0:ROWS, 0:ROWS])
            ins.then_inc(psum_full, 1)
            pe.get()
            for _ in range(4):
                pe_features(pe, xT)
            for _ in range(6):
                pe_tokens(pe, xT)
            pe_product(pe, xT)
            pe.get()
            for t in range(T):
                for c in range(0, DC, 4):
                    b = pe.q.fill()
                    for k in range(4):
                        ins = tr(ps[b][:, k * P:(k + 1) * P], acc[:, c + k, t * P:(t + 1) * P],
                                 ident[:])
                    ins.then_inc(psum_full, 1)
            pe_product(pe, xT)
            pe.get()
            for i in range(2):
                pe_to_features(pe, lambda c, t: qk[:, i * T + t].rearrange(
                    "p m d -> p (m d)")[:, c * P:(c + 1) * P], HEADS)
            pe.get()
            pe_to_features(pe, lambda c, t: convT[:, t, c * P:(c + 1) * P], DC)
            pe.get()
            for n in range(2):
                pe_tokens(pe, acc, bias=(ident[:, 6:7].to_broadcast([P, P]),
                                         bias_rows[:, n * 512:(n + 1) * 512]))
            for t in range(T):
                kw = (t + 1) * P
                for maps in bank_heads(t, MAPS):
                    b = pe.q.fill()
                    for k, m in enumerate(maps):
                        r = slice(HD * (m % 2), HD * (m % 2 + 1))
                        ins = mm(ps[b][:, k * kw:(k + 1) * kw],
                                 qT[r, m // 2, t * P:(t + 1) * P], kT[r, m // 2, 0:kw],
                                 start=True, stop=True)
                    ins.then_inc(psum_full, 1)
            for t in range(T):
                pe.get()
                blocks = [(hd, k) for hd in range(HEADS) for k in range(t + 1)]
                for i in range(0, len(blocks), 4):
                    b = pe.q.fill()
                    for n, (hd, k) in enumerate(blocks[i:i + 4]):
                        ins = tr(ps[b][:, n * P:(n + 1) * P],
                                 tiles[t][:, 2 * hd, k * P:(k + 1) * P], ident[:])
                    ins.then_inc(psum_full, 1)
                pe.get()
                for h0 in range(0, HEADS, 4):
                    b = pe.q.fill()
                    for n in range(4):
                        hd = h0 + n
                        for k in range(t + 1):
                            ins = mm(ps[b][:, n * P:(n + 1) * P], softT[:, (t + 1) * hd + k, :],
                                     val[:, k, hd * P:(hd + 1) * P], start=k == 0, stop=k == t)
                    ins.then_inc(psum_full, 1)
            pe_mod(pe, GATE1)
            pe.get()
            pe_to_features(pe, strided(y_attn), DC)
            pe.get()
            pe_product(pe, xT)

        def vec_part(v):
            e, do = v.eng, v.do
            tt, ts, cp, stt = e.tensor_tensor, e.tensor_scalar, e.tensor_copy, \
                e.scalar_tensor_tensor
            v.ask()
            v.answer()
            v.feed()
            for i in range(8):
                f = float(np.float32(THETA) ** np.float32(-2.0 * i / ROT))
                do(e.memset(inv_freq[:, i:i + 1], f))
            do(cp(pos, pos_i[:]))
            for t in range(T):
                do(ts(ang[:, 0, t], inv_freq, pos[:, t:t + 1], None, ALU.mult))
            do(cp(ang[:, 1], ang[:, 0]))
            do(ts(turns[:, 0], ang[:, 0], 1.0 / (2 * math.pi), None, ALU.mult))
            do(ts(turns[:, 1], ang[:, 1], 1.0 / (2 * math.pi), 0.25, ALU.mult, ALU.add))
            do(ts(turns, turns, 1.5 * 2 ** 23, None, ALU.add))
            do(ts(turns, turns, -1.5 * 2 ** 23, None, ALU.add))
            left = 2 * math.pi
            for bits in (2.0 ** -5, 2.0 ** -15, None):
                part = float(np.float32(left)) if bits is None else round(left / bits) * bits
                left -= part
                do(stt(ang, turns, -part, ang, ALU.mult, ALU.add))
            do(ts(ang[:, 1], ang[:, 1], math.pi / 2, None, ALU.add))
            top = float(np.nextafter(np.float32(math.pi), np.float32(0)))
            do(ts(ang, ang, top, -top, ALU.min, ALU.max))
            for i in range(2):
                a_, b_ = (lams[:, (2 * i + j) * HD:(2 * i + j + 1) * HD] for j in range(2))
                do(tt(a_, a_, b_, ALU.mult))
                do(e.tensor_reduce(lam[:, i:i + 1], a_, AX.X, ALU.add))
            v.ask()
            v.answer()
            do(tt(lam[:, 2:3], lam[:, 1:2], lam[:, 0:1], ALU.subtract))
            do(ts(lam[:, 2:3], lam[:, 2:3], -LAMBDA0, None, ALU.add))
            vec_ada_norm(v, scale1, shift1)
            vec_to_features(v, xT, DC, tell=False)
            b = v.q.take()
            do(cp(taps, view(ps[b], 0, (DC, ROWS))), psum_free)
            v.feed()
            do(e.memset(u[:, :, 0:TAPS - 1], 0.0))
            for c in range(0, DC, 2):
                b = v.q.take()
                do(cp(acc[:, c:c + 2, :], view(ps[b], 0, (2, S))), psum_free)
            for c in range(0, DC, 2):
                b = v.q.take()
                do(cp(u[:, c:c + 2, TAPS - 1:], view(ps[b], 0, (2, S))), psum_free)
            v.ask()
            v.answer()
            do(tt(u[:, :, TAPS - 1:], u[:, :, TAPS - 1:], acc, ALU.mult))

            steps = [(i, c) for i in range(TAPS) for c in range(DC)]
            done = [0]

            def convolve(n):
                for i, c in steps[done[0]:done[0] + n]:
                    src = u[:, c, i:i + S]
                    if i == 0:
                        ins = ts(acc[:, c, :], src, taps[:, c, 0:1], dw_b[:, c:c + 1],
                                 ALU.mult, ALU.add)
                    else:
                        e.wait_ge(conv_step, done[0] - DC + 1)
                        ins = stt(acc[:, c, :], src, taps[:, c, i:i + 1], acc[:, c, :],
                                  ALU.mult, ALU.add)
                    ins.then_inc(conv_step, 1)
                    done[0] += 1

            for i in range(3):
                for n in range(2):
                    for t in range(T):
                        b = v.q.take()
                        if i < 2:
                            dst = qk[:, i * T + t, n * 8:(n + 1) * 8, :]
                            do(cp(dst, view(ps[b], 0, (8, HD))), psum_free)
                        else:
                            do(cp(val[:, t, n * 512:(n + 1) * 512], ps[b][:]), psum_free)
                        convolve(21)
            assert done[0] == len(steps)
            e.wait_ge(conv_step, len(steps))
            v.feed()
            do(tt(sq, qk, qk, ALU.mult))
            do(e.tensor_reduce(ss, sq, AX.X, ALU.add))
            v.ask()
            v.answer()
            do(e.reciprocal(ss, ss))
            for i in range(2 * T):
                x = qk[:, i]
                do(tt(x, x, along(ss[:, i], HD), ALU.mult))
                do(tt(x, x, every(qg if i < T else kg, MAPS), ALU.mult))
                sin, cos = (every(trig[:, j, i % T], MAPS) for j in range(2))
                x1, x2 = x[:, :, 0:8], x[:, :, 8:16]
                do(tt(rot_a[:, i], x1, sin, ALU.mult))
                do(tt(rot_b[:, i], x2, sin, ALU.mult))
                do(tt(x1, x1, cos, ALU.mult))
                do(tt(x2, x2, cos, ALU.mult))
                do(tt(x1, x1, rot_b[:, i], ALU.subtract))
                do(tt(x2, x2, rot_a[:, i], ALU.add))
            v.feed()

            def gate_to_dram():
                for _ in range(4):
                    v.hand()
                v.ask()
                v.answer()
                v.give_back(4)

            gate_to_dram()
            for t in range(T):
                for c in range(0, D, 512):
                    b = v.q.take()
                    do(cp(convT[:, t, c:c + 512], ps[b][:]), psum_free)
            do(e.tensor_reduce(mean, convT[:], AX.X, ALU.add))
            do(ts(mean, mean, 1.0 / D, None, ALU.mult))
            for t in range(T):
                do(ts(convT[:, t], convT[:, t], mean[:, t:t + 1], None, ALU.subtract))
            v.ask()
            v.answer()
            do(e.reciprocal(var, var))
            for t in range(T):
                do(ts(convT[:, t], convT[:, t], var[:, t:t + 1], None, ALU.mult))
            gate_to_dram()
            vec_to_features(v, qT, HEADS, tell=False)
            vec_to_features(v, kT, HEADS, tell=False)
            v.feed()
            for c in range(0, DC, 2):
                v.hand()
            v.ask()
            v.answer()
            v.give_back(4)
            v.feed()
            for n in range(2):
                for t in range(T):
                    b = v.q.take()
                    do(cp(convT[:, t, n * 512:(n + 1) * 512], ps[b][:]), psum_free)
            e.wait_ge(gate_stored, 32)
            for t in range(T):
                kw = (t + 1) * P
                for maps in bank_heads(t, MAPS):
                    b = v.q.take()
                    m0 = maps[0]
                    do(cp(tiles[t][:, m0:maps[-1] + 1:2, :], view(ps[b], 0, (len(maps), kw))),
                       psum_free)
                diag = tiles[t][:, :, t * P:kw]
                do(tt(diag, diag, every(causal[:], MAPS), ALU.add))
                do(e.tensor_reduce(mx[:, t], tiles[t], AX.X, ALU.max))
                do(ts(mx[:, t], mx[:, t], -HD ** -0.5, None, ALU.mult))
                v.ask()
            for t in range(T):
                kw = (t + 1) * P
                v.answer()
                do(e.reciprocal(den[:, t], den[:, t]))
                do(ts(den[:, t, 1::2], den[:, t, 1::2], lam[:, 2:3], None, ALU.mult))
                do(tt(tiles[t], tiles[t], along(den[:, t], kw), ALU.mult))
                do(tt(tiles[t][:, 0::2, :], tiles[t][:, 0::2, :], tiles[t][:, 1::2, :], ALU.add))
                v.feed()
                for i in range(0, HEADS * (t + 1), 4):
                    b = v.q.take()
                    do(cp(softT[:, i:i + 4, :], view(ps[b], 0, (4, P))), psum_free)
                v.feed()
                for c in range(0, D, 512):
                    b = v.q.take()
                    do(cp(y_attn[:, t, c:c + 512], ps[b][:]), psum_free)
            v.ask()
            for t in range(T):
                heads = y_attn[:, t].rearrange("p (h d) -> p h d", h=HEADS)
                scratch = gate_stage[:, t].rearrange("p (h d) -> p h d", h=HEADS)
                do(tt(scratch, heads, heads, ALU.mult))
                do(e.tensor_reduce(oss[:, t], scratch, AX.X, ALU.add))
            v.ask()
            v.answer()
            do(e.reciprocal(oss, oss))
            do(ts(oss, oss, 1.0 - LAMBDA0, None, ALU.mult))
            for t in range(T):
                heads = y_attn[:, t].rearrange("p (h d) -> p h d", h=HEADS)
                do(tt(heads, heads, along(oss[:, t], P), ALU.mult))
                do(tt(heads, heads, every(sub_g, HEADS), ALU.mult))
            e.wait_ge(gate_back, 32)
            do(tt(convT[:], convT[:], gate_conv, ALU.mult))
            do(tt(y_attn, y_attn, gate_attn, ALU.mult))
            do(tt(y_attn, y_attn, convT[:], ALU.add))
            v.feed()
            vec_mod(v, gate1)
            vec_to_features(v, xT, DC, tell=False)
            v.feed()
            got = [v.q.take() for _ in range(4)]
            vec_gated_product(v, lambda t, n: ps[got[2 * n + t]], gate1)
            v.give_back(4)
            e.sem_inc(arena_free, 1)

        def act_part(a):
            f, do = a.eng.activation, a.do
            a.get()
            do(f(cT[:], cT[:], ACT.Silu))
            a.put()
            a.get()
            do(f(lam[:, 0:2], lam[:, 0:2], ACT.Exp))
            do(f(trig, ang, ACT.Sin))
            a.put()
            act_norm(a, h)
            a.get()
            do(f(u[:, :, TAPS - 1:], u[:, :, TAPS - 1:], ACT.Sigmoid))
            a.put()
            a.get()
            do(f(ss, ss, ACT.Sqrt, bias=eps[:], scale=1.0 / HD))
            a.put()
            gate_to_dram(a, 0)
            a.get()
            for t in range(T):
                do(f(gate_scratch[:], convT[:, t], ACT.Square, accum_out=var[:, t:t + 1]))
            do(f(var, var, ACT.Sqrt, bias=eps[:], scale=1.0 / D))
            a.put()
            gate_to_dram(a, 1)
            a.get()
            for c in range(0, DC, 2):
                bank = a.bank()
                for k in range(2):
                    do(f(acc[:, c + k, :], bank[:, k * S:(k + 1) * S], ACT.Silu,
                         bias=ln_b[:, c + k:c + k + 1], scale=ln_g[:, c + k:c + k + 1]))
            a.put()
            for t in range(T):
                a.get()
                if t == T - 1:
                    a.eng.dma_start(gate_conv, hybrid_gates[0]).then_inc(gate_back, 16)
                for m in range(MAPS):
                    do(f(tiles[t][:, m, :], tiles[t][:, m, :], ACT.Exp, scale=HD ** -0.5,
                         bias=mx[:, t, m:m + 1], accum_out=den[:, t, m:m + 1]))
                a.put()
            a.get()
            a.eng.dma_start(gate_attn, hybrid_gates[1]).then_inc(gate_back, 16)
            a.get()
            do(f(oss, oss, ACT.Sqrt, bias=eps[:], scale=1.0 / P))
            a.put()

        def gate_to_dram(a, i):
            a.get()
            if i:
                a.eng.wait_ge(gate_stored, 16)
            for n in range(2):
                for t in range(T):
                    a.do(a.eng.activation(gate_stage[:, t, n * 512:(n + 1) * 512], a.bank()[:],
                                          ACT.Sigmoid))
            a.put()
            a.eng.dma_start(hybrid_gates[i], gate_stage).then_inc(gate_stored, 16)

        gate_scratch = view(arena, qk_T0 + HEADS * S, (D,))

        def sp_part(sp):
            sp_mod(sp, SCALE1)
            sp_mod(sp, SHIFT1)
            for lo in range(0, 7 * D, 512):
                sp.project("w_in_2", lo)
            for lo in (0, 512):
                sp.project("w_pw2_2", lo, natural=True)
            sp_mod(sp, GATE1)
            for lo in (0, 512):
                sp.project("w_out_2", lo)
        return (pe_part, vec_part, act_part, sp_part), pool_part

    if "E" in STAGES:
        STAGE_PARTS["E"], pool_E = hybrid()

    def experts():
        GROUPS, PER, TOP_GROUPS, SCALE = 8, 8, 4, 2.5
        router, e = carve(ff_end, DC, N_EXP)
        gate2 = gainb[(len(gain_order)) % 2][:]
        scale2, e = carve(e, D)
        shift2, e = carve(e, D)
        gates, e = carve(e, T, N_EXP)
        scores, e = carve(e, T, N_EXP)
        choice, e = carve(e, T, N_EXP)
        left, e = carve(e, T, N_EXP)
        best, e = carve(e, T, GROUPS, 8)
        more, e = carve(e, T, GROUPS, GROUPS)
        gatesT, e = carve(e, S)
        bias64, e = carve(e, N_EXP)
        assert e <= BIAS0
        gsum, rank, total = view(sm, 0, (T, GROUPS)), view(sm, 16, (T, GROUPS)), \
            view(sm, 32, (T,))
        router_loaded, gates_stored = sem("router_loaded"), sem("gates_stored")
        gate_loaded = [sem(f"gate_row_loaded{i}") for i in range(NS)]
        hidden_set = ff_sems("moe")[2]
        NB = N_EXP + 1
        base = []

        def pool_part(eng, g, load_bias):
            if not load_bias:
                eng.wait_ge(arena_free, 1)
            if load_bias:
                g(eng.memset(bias_rows, 0.0))
                eng.dma_start(bias_rows[0:6], A["b_ada_2"].rearrange("l (j n) -> (l j) n", j=6))\
                   .then_inc(bias_loaded, 16)
                eng.dma_start(bias_rows[6:7], A["b_pw2_2"]).then_inc(bias_loaded, 16)
            eng.dma_start(router, weight("w_router_2").rearrange("(p c) n -> p c n", c=DC))\
               .then_inc(router_loaded, 16)
            eng.dma_start(bias64, A["router_bias_2"][0].partition_broadcast(P))\
               .then_inc(router_loaded, 16)
            eng.wait_ge(gates_stored, 16)

            def gate_row(x, slot):
                eng.dma_start(gate_rows[:, slot, :].unsqueeze(1),
                              gates_dram[bass.ds(x, 1), :].partition_broadcast(P))\
                   .then_inc(gate_loaded[slot], 16)

            for x in range(NS):
                gate_row(x, x)
            with eng.Fori(0, N_EXP // NS - 1) as j:
                for i in range(NS):
                    eng.wait_ge(hidden_set, 2 * (NS * j + i + 1) + 2)
                    gate_row(NS * j + NS + i, i)

        def pe_part(pe):
            mm, tr = pe.eng.matmul, pe.eng.transpose
            pe.get()
            pe.eng.wait_ge(bias_loaded, 32)
            pe_mod(pe, SCALE2)
            pe_mod(pe, SHIFT2)
            pe_mod(pe, GATE2, (0,))
            pe.get()
            pe_to_features(pe, strided(xn), DC)
            pe.get()
            pe.eng.wait_ge(router_loaded, 32)
            b = pe.q.fill()
            for t in range(T):
                for c in range(DC):
                    ins = mm(ps[b][:, t * N_EXP:(t + 1) * N_EXP], xT[:, c, t * P:(t + 1) * P],
                             router[:, c, :], start=c == 0, stop=c == DC - 1)
            ins.then_inc(psum_full, 1)
            pe_mod(pe, GATE2, (1,))
            pe.get()
            b = pe.q.fill()
            for t in range(T):
                ins = tr(ps[b][0:N_EXP, t * P:(t + 1) * P], gates[:, t, :], ident[:])
            ins.then_inc(psum_full, 1)
            base.append(pe.block)
            pe_ff(pe, "moe", NB)

        def vec_part(v):
            e, do = v.eng, v.do
            tt, ts, cp = e.tensor_tensor, e.tensor_scalar, e.tensor_copy
            if "E" not in STAGES:
                v.ask()
                v.answer()
            v.feed()
            vec_norm(v, h)
            g = v.gain()
            for n in range(2):
                at = slice(n * 512, (n + 1) * 512)
                b = v.q.take()
                do(e.scalar_tensor_tensor(scale2[:, at], ps[b][:], 1.0, g[:, at],
                                          ALU.add, ALU.mult), psum_free)
            vec_mod(v, shift2)
            for t in range(T):
                do(tt(xn[:, t], xn[:, t], scale2, ALU.mult))
                do(tt(xn[:, t], xn[:, t], shift2, ALU.add))
            v.feed()
            b = v.q.take()
            do(cp(gate2[:, 0:512], ps[b][:]), psum_free)
            vec_to_features(v, xT, DC)
            b = v.q.take()
            do(cp(left, view(ps[b], 0, (T, N_EXP))), psum_free)
            v.ask()
            v.answer()
            e.wait_ge(router_loaded, 32)
            do(tt(choice, scores, every(bias64, T), ALU.add))
            for t in range(T):
                for g_ in range(GROUPS):
                    do(e.max(best[:, t, g_, :], choice[:, t, g_ * PER:(g_ + 1) * PER]))
            do(tt(gsum, best[:, :, :, 0], best[:, :, :, 1], ALU.add))
            for t in range(T):
                mine, other = along(gsum[:, t], GROUPS), every(gsum[:, t], GROUPS)
                do(tt(more[:, t], other, mine, ALU.is_equal))
                do(tt(more[:, t], more[:, t], earlier[:], ALU.mult))
                do(tt(left[:, t].rearrange("p (a b) -> p a b", a=GROUPS), other, mine, ALU.is_gt))
                do(tt(more[:, t], more[:, t],
                      left[:, t].rearrange("p (a b) -> p a b", a=GROUPS), ALU.add))
            do(e.tensor_reduce(rank, more, AX.X, ALU.add))
            do(ts(rank, rank, TOP_GROUPS - 0.5, NEG, ALU.is_gt, ALU.mult))
            for t in range(T):
                by_group = choice[:, t].rearrange("p (g e) -> p g e", g=GROUPS)
                do(tt(by_group, by_group, along(rank[:, t], PER), ALU.add))
                do(e.max(best[:, t, 0, :], choice[:, t]))
                do(e.match_replace(left[:, t], best[:, t, 0, :], choice[:, t], 2 * NEG))
            do(tt(left, left, choice, ALU.not_equal))
            do(tt(gates, scores, left, ALU.mult))
            do(e.tensor_reduce(total, gates, AX.X, ALU.add))
            do(e.reciprocal(total, total))
            do(ts(total, total, SCALE, None, ALU.mult))
            do(tt(gates, gates, along(total, N_EXP), ALU.mult))
            v.feed()
            b = v.q.take()
            do(cp(gate2[:, 512:D], ps[b][:]), psum_free)
            b = v.q.take()
            do(cp(gatesT[0:N_EXP], ps[b][0:N_EXP, 0:S]), psum_free)
            v.ask()
            vec_cut_x(v)
            e.wait_ge(gates_stored, 16)
            vec_ff(v, "moe", NB, base[0], gate_loaded)
            vec_gated_product(v, ff_bank, gate2)

        def act_part(a):
            if "E" not in STAGES:
                a.get()
                a.do(a.eng.activation(cT[:], cT[:], ACT.Silu))
                a.put()
            act_norm(a, h)
            a.get()
            a.do(a.eng.activation(scores, left, ACT.Sigmoid))
            a.put()
            a.get()
            a.eng.dma_start(gates_dram, gatesT[0:N_EXP]).then_inc(gates_stored, 16)
            a.eng.wait_ge(gates_stored, 16)
            act_ff(a, "moe", NB, base[0])

        def sp_part(sp):
            sp_mod(sp, SCALE2)
            sp_mod(sp, SHIFT2)
            sp_mod(sp, GATE2)
            gu = A["w_exp_gu_2"].rearrange("l e (p c) n -> (l e) p c n", c=DC)
            dn = A["w_exp_down_2"].rearrange("l e (f p) n -> (l e) p f n", p=P)

            def parts(x):
                return lambda s: [
                    (wide[s][:, 0:4, :].unsqueeze(1),
                     gu[bass.ds(x, 1), :, 0:4, :].rearrange("e p c n -> p e c n")),
                    (wide[s][:, 4:8, :].unsqueeze(1),
                     gu[bass.ds(x, 1), :, 4:8, :].rearrange("e p c n -> p e c n")),
                    (down[s].unsqueeze(1), dn[bass.ds(x, 1)].rearrange("e p f n -> p e f n"))]

            sg = weight("w_sh_gu_2").rearrange("(p c) n -> p c n", c=DC)
            sd = weight("w_sh_down_2").rearrange("(f p) n -> p f n", p=P)
            sp.load(lambda s: [(wide[s][:, 0:4, :], sg[:, 0:4, :]),
                               (wide[s][:, 4:8, :], sg[:, 4:8, :]), (down[s], sd)])
            for b in range(1, NS):
                sp.load(parts(b - 1))
            low_set = ff_weight_sems("moe")[1]
            with sp.eng.Fori(0, N_EXP // NS - 1) as j:
                for i in range(NS):
                    sp.eng.wait_ge(low_set[2], NS * j + i + 1)
                    s = (base[0] + i) % NS
                    for dst, src in parts(NS * j + NS + i - 1)(s):
                        sp.eng.dma_start(dst, src).then_inc(loaded[s], 16)
            sp.block += N_EXP - NS
            sp.load(parts(N_EXP - 1))
        return (pe_part, vec_part, act_part, sp_part), pool_part

    if "F" in STAGES:
        STAGE_PARTS["F"], pool_F = experts()

    stages = [STAGE_PARTS[x] for x in STAGES]
    block = ctx.enter_context(nc.Block())

    @block.tensor
    def _(eng):
        pe = Pe(eng)
        eng.wait_ge(consts, 1)
        for i, (pe_part, _, _, _) in enumerate(stages):
            if i == min(1, len(stages) - 1):
                eng.wait_ge(consts, 2)
                eng.wait_ge(params_loaded, 16 * (len(params) - PRE_GAINS))
            pe_part(pe)

    @block.vector
    def _(eng):
        v = Vec(eng)
        eng.wait_ge(consts, 1)
        eng.wait_ge(x_loaded, 16)
        eng.wait_ge(gains_loaded, 16 * PRE_GAINS)
        for i, (_, vec_part, _, _) in enumerate(stages):
            if i == min(1, len(stages) - 1):
                eng.wait_ge(consts, 2)
                eng.wait_ge(params_loaded, 16 * (len(params) - PRE_GAINS))
            vec_part(v)
        v.ask()

    @block.scalar
    def _(eng):
        a = Act(eng)
        for i, (dst, src) in enumerate(params):
            eng.dma_start(dst, src, allow_slow_non_contiguous=True)\
               .then_inc(gains_loaded if i < PRE_GAINS else params_loaded, 16)
        eng.wait_ge(consts, 1)
        for i, (_, _, act_part, _) in enumerate(stages):
            if i == min(1, len(stages) - 1):
                eng.wait_ge(consts, 2)
                eng.wait_ge(params_loaded, 16 * (len(params) - PRE_GAINS))
            act_part(a)
        a.get()
        eng.dma_start(out.rearrange("b (t p) d -> p (b t) d", p=P), h[:]).then_inc(out_done, 16)
        eng.wait_ge(out_done, 16)

    @block.gpsimd
    def _(eng):
        g = Steps(eng, g_step)

        def select(ap, pattern, base, mult, op, fill):
            g(eng.affine_select(out=ap, in_=ap, pattern=pattern, compare_op=op, fill=fill,
                                base=base, channel_multiplier=mult))

        half = slice(0, P // 2)
        rest = slice(P // 2, P)
        g(eng.memset(eps[:], EPS))
        g(eng.memset(ident[:], 0.0))
        select(ident[:], [[-1, P]], 0, 1, ALU.not_equal, 1.0)
        eng.sem_inc(consts, 1)
        g(eng.memset(tri1[:], 1.0))
        select(tri, [[1, P]], 0, -1, ALU.is_ge, 0.0)
        g(eng.memset(tri_chunk[:], 1.0))
        select(tri_chunk[:], [[1, P]], 0, -1, ALU.is_ge, 0.0)
        g(eng.memset(tri_chunk[half, rest], 0.0))
        g(eng.memset(ones_chunk[:], 0.0))
        g(eng.memset(ones_chunk[half, half], 1.0))
        g(eng.memset(ones_chunk[rest, rest], 1.0))
        g(eng.memset(causal[:], 0.0))
        select(causal[:], [[-1, P]], 0, 1, ALU.is_ge, NEG)
        g(eng.memset(causal_chunk[:], 0.0))
        select(causal_chunk[:], [[1, P]], 0, -1, ALU.is_ge, NEG)
        g(eng.memset(causal_chunk[half, rest], NEG))
        g(eng.memset(earlier[:], 1.0))
        select(earlier[:], [[1, 8], [-1, 8]], 0, 0, ALU.is_gt, 0.0)
        g(eng.memset(levels[:], 0.0))
        for k in range(LEVELS):
            w = 1 << k
            part = levels[:, k, :].rearrange("p (i c) -> p i c", c=2 * w)[:, :, w:2 * w]
            g(eng.memset(part, 1.0))
            select(part, [[-2 * w, P // (2 * w)], [0, w]], 0, 1, ALU.is_ge, 0.0)
            select(part, [[2 * w, P // (2 * w)], [0, w]], w, -1, ALU.is_gt, 0.0)
        eng.sem_inc(consts, 1)
        for k, name in enumerate(gain_order):
            if k >= 2:
                eng.wait_ge(gain_used, k - 1)
            eng.dma_start(gainb[k % 2][:], A[name][0].partition_broadcast(P))\
               .then_inc(gain_loaded[k % 2], 16)
        if "E" in STAGES:
            pool_E(eng, g, gain_order.index("norm1_g_2"))
        if "F" in STAGES:
            pool_F(eng, g, "E" not in STAGES)

    @block.sync
    def _(eng):
        sp = Sp(eng)
        eng.dma_start(h[:], A["x"].rearrange("b (t p) d -> p (b t) d", p=P)).then_inc(x_loaded, 16)
        for _, _, _, sp_part in stages:
            sp_part(sp)


def kernel(**inputs):
    import concourse.bacc as bacc
    from concourse.bass_utils import run_bass_kernel_spmd

    nc = bacc.Bacc("TRN2", target_bir_lowering=False, num_devices=1)
    arrays, aps = {}, {}
    for name, value in inputs.items():
        a = np.ascontiguousarray(value)
        arrays[f"in_{name}"] = a
        aps[name] = nc.dram_tensor(f"in_{name}", a.shape, mybir.dt.from_np(a.dtype),
                                   kind="ExternalInput").ap()
    out = nc.dram_tensor("out", inputs["x"].shape, F32, kind="ExternalOutput").ap()
    build(nc, aps, out)
    return run_bass_kernel_spmd(nc, [arrays], core_ids=[0]).results[0]["out"]
```
